# Optimizing a Trainium2 kernel written in Bass

```python
import jax, jax.numpy as jnp
from jax import lax
import numpy as np

D_MODEL = 2048
BATCH = 1
SEQ = 512
DEPTH = 1
DEC_BATCH = 8
DEC_SEQ = 4
PAST_LEN = 1024
PAGE_SIZE = 128

N_HEADS = 8
N_KV_HEADS = 2
GQA = N_HEADS // N_KV_HEADS
HEAD_DIM = 128
ATTN_W = N_HEADS * HEAD_DIM
KV_W = N_KV_HEADS * HEAD_DIM
GATE_COLS = 3 * N_HEADS
BLOCK_CMP = 32
STRIDE_CMP = 16
CMP_HID = 256
SEL_BLOCK = 64
TOP_N = 16
WINDOW = 512
Q_BLOCK = 128
CONV_CH = D_MODEL - ATTN_W
CONV_W = 31
IN_COLS = ATTN_W + 6 * KV_W + GATE_COLS + 2 * CONV_CH
D_FF = 5632
FFN_CONV_W = 3
N_MEM = 256
MEM_HEADS = 4
MEM_HEAD_DIM = 128
MEM_W = MEM_HEADS * MEM_HEAD_DIM
ATTN_SCALE = HEAD_DIM ** -0.5
MEM_SCALE = MEM_HEAD_DIM ** -0.5
EPS = 1e-6

kernel_name = 'hymba_nsa_conformer_step'

def rmsnorm(x, g):
    xf = x.astype(jnp.float32)
    y = xf * lax.rsqrt(jnp.mean(xf * xf, axis=-1, keepdims=True) + EPS)
    return y.astype(x.dtype) * g

def layernorm(x, g, b):
    xf = x.astype(jnp.float32)
    mu = jnp.mean(xf, axis=-1, keepdims=True)
    var = jnp.mean(jnp.square(xf - mu), axis=-1, keepdims=True)
    return ((xf - mu) * lax.rsqrt(var + EPS)).astype(x.dtype) * g + b

def masked_softmax(s, mask):
    s = jnp.where(mask, s.astype(jnp.float32), -jnp.inf)
    m = jnp.max(s, axis=-1, keepdims=True)
    m = jnp.where(jnp.isfinite(m), m, 0.0)
    e = jnp.where(mask, jnp.exp(s - m), 0.0)
    return e / jnp.maximum(jnp.sum(e, axis=-1, keepdims=True), 1e-30)

def causal_dwconv(ext, w, b):
    y = lax.conv_general_dilated(ext, w[:, None, :].astype(ext.dtype), window_strides=(1,), padding='VALID',
                                 dimension_numbers=('NWC', 'WIO', 'NWC'), feature_group_count=ext.shape[-1])
    return y + b

def project(h, w_in, b_gate):
    B, T, _ = h.shape
    sizes = [ATTN_W] + [KV_W] * 6 + [GATE_COLS, 2 * CONV_CH]
    q, kc, vc, ks, vs, kw, vw, g, glu = jnp.split(h @ w_in, np.cumsum(sizes)[:-1].tolist(), axis=-1)
    kv = lambda a: a.reshape(B, T, N_KV_HEADS, HEAD_DIM)
    q = q.reshape(B, T, N_KV_HEADS, GQA, HEAD_DIM).transpose(0, 2, 3, 1, 4)
    gates = jax.nn.sigmoid(g + b_gate).reshape(B, T, N_KV_HEADS, GQA, 3).transpose(0, 2, 3, 1, 4)
    return q, kv(kc), kv(vc), kv(ks), kv(vs), kv(kw), kv(vw), gates, glu

def compress(rows, pe, w1, b1, w2):
    B, L, KV, DH = rows.shape
    n_chunk = L // STRIDE_CMP
    c = rows[:, :n_chunk * STRIDE_CMP].reshape(B, n_chunk, STRIDE_CMP, KV, DH)
    w1r = w1.reshape(BLOCK_CMP, DH, CMP_HID)
    lead = jnp.einsum('bnlkd,ldf->bnkf', c + pe[:STRIDE_CMP, None, :], w1r[:STRIDE_CMP])
    trail = jnp.einsum('bnlkd,ldf->bnkf', c + pe[STRIDE_CMP:, None, :], w1r[STRIDE_CMP:])
    hid = jax.nn.gelu(lead[:, :-1] + trail[:, 1:] + b1)
    return jnp.einsum('bnkf,fd->bnkd', hid, w2)

def to_blocks(rows, n_sel):
    B, L, KV, DH = rows.shape
    rows = jnp.pad(rows, ((0, 0), (0, n_sel * SEL_BLOCK - L), (0, 0), (0, 0)))
    return rows.reshape(B, n_sel, SEL_BLOCK, KV, DH).transpose(0, 3, 1, 2, 4)

def compressed_attention(q, q_pos, kcc, vcc):
    end = jnp.arange(kcc.shape[1]) * STRIDE_CMP + (BLOCK_CMP - 1)
    mask = end[None, :] <= q_pos[:, None]
    s = jnp.einsum('bkgtd,bnkd->bkgtn', q, kcc) * ATTN_SCALE
    p = masked_softmax(s, mask)
    return jnp.einsum('bkgtn,bnkd->bkgtd', p.astype(vcc.dtype), vcc), p

def select_blocks(p_cmp, q_pos, n_sel):
    i = jnp.arange(p_cmp.shape[-1])[:, None] * STRIDE_CMP
    j = jnp.arange(n_sel)[None, :] * SEL_BLOCK
    overlap = jnp.clip(jnp.minimum(i + BLOCK_CMP, j + SEL_BLOCK) - jnp.maximum(i, j), 0, None).astype(jnp.float32) / BLOCK_CMP
    imp = jnp.einsum('bkgtn,ns->bkts', p_cmp, overlap)
    blk = jnp.arange(n_sel)[None, :]
    cur = (q_pos // SEL_BLOCK)[:, None]
    valid = blk * SEL_BLOCK <= q_pos[:, None]
    forced = (blk == 0) | (blk == cur) | (blk == cur - 1)
    score = jnp.where(valid, jnp.where(forced, jnp.inf, imp), -jnp.inf)
    _, idx = lax.top_k(score, min(TOP_N, n_sel))
    return idx

def selected_attention(q, q_pos, idx, kb, vb):
    gather = jax.vmap(jax.vmap(lambda blocks, sel: blocks[sel]))
    kg, vg = gather(kb, idx), gather(vb, idx)
    B, KV, Tq, K, SB, DH = kg.shape
    kg, vg = kg.reshape(B, KV, Tq, K * SB, DH), vg.reshape(B, KV, Tq, K * SB, DH)
    k_pos = (idx[..., None] * SEL_BLOCK + jnp.arange(SEL_BLOCK)).reshape(B, KV, Tq, K * SB)
    mask = (k_pos <= q_pos[:, None])[:, :, None]
    s = jnp.einsum('bkgtd,bktsd->bkgts', q, kg) * ATTN_SCALE
    p = masked_softmax(s, mask)
    return jnp.einsum('bkgts,bktsd->bkgtd', p.astype(vg.dtype), vg)

def cmp_and_select(q, q_pos, kcc, vcc, kb, vb):
    o_c, p_c = compressed_attention(q, q_pos, kcc, vcc)
    idx = select_blocks(p_c, q_pos, kb.shape[2])
    return o_c, selected_attention(q, q_pos, idx, kb, vb)

def window_attention(q, q_pos, k, v, k_pos):
    kp, qp = k_pos[:, None, :], q_pos[:, :, None]
    mask = (kp <= qp) & (qp - kp < WINDOW) & (kp >= 0)
    s = jnp.einsum('bkgntd,bnskd->bkgnts', q, k) * ATTN_SCALE
    p = masked_softmax(s, mask)
    return jnp.einsum('bkgnts,bnskd->bkgntd', p.astype(v.dtype), v)

def banded_window_attention(q, kw, vw):
    B, KV, G, T, DH = q.shape
    nb, nprev = T // Q_BLOCK, WINDOW // Q_BLOCK

    def band(rows):
        padded = jnp.concatenate([jnp.zeros((B, WINDOW, KV, DH), rows.dtype), rows], axis=1)
        blocks = padded.reshape(B, nb + nprev, Q_BLOCK, KV, DH)
        return jnp.concatenate([blocks[:, i:i + nb] for i in range(nprev + 1)], axis=2)

    k_pos = jnp.arange(nb)[:, None] * Q_BLOCK - WINDOW + jnp.arange((nprev + 1) * Q_BLOCK)[None, :]
    q_pos = jnp.arange(T).reshape(nb, Q_BLOCK)
    o = window_attention(q.reshape(B, KV, G, nb, Q_BLOCK, DH), q_pos, band(kw), band(vw), k_pos)
    return o.reshape(B, KV, G, T, DH)

def conformer_conv(glu_in, prev, conv_w, conv_b, ln_g, ln_b):
    a, gate = jnp.split(glu_in, 2, axis=-1)
    u = a * jax.nn.sigmoid(gate)
    ext = jnp.concatenate([prev, u], axis=1)
    y = jax.nn.silu(layernorm(causal_dwconv(ext, conv_w, conv_b), ln_g, ln_b))
    return y, ext[:, ext.shape[1] - (CONV_W - 1):]

def memory_kv(mem, mem_norm_g, w_mk, w_mv):
    B = mem.shape[0]
    m = rmsnorm(mem, mem_norm_g)
    return (m @ w_mk).reshape(B, N_MEM, MEM_HEADS, MEM_HEAD_DIM), (m @ w_mv).reshape(B, N_MEM, MEM_HEADS, MEM_HEAD_DIM)

def memory_attention(h, mk, mv, w_mq, w_mo):
    B, T, _ = h.shape
    q = (h @ w_mq).reshape(B, T, MEM_HEADS, MEM_HEAD_DIM)
    s = jnp.einsum('bthd,bmhd->bhtm', q, mk).astype(jnp.float32) * MEM_SCALE
    p = jax.nn.softmax(s, axis=-1).astype(mv.dtype)
    return jnp.einsum('bhtm,bmhd->bthd', p, mv).reshape(B, T, MEM_W) @ w_mo

def conv_ffn(h, prev, w_gate, w_up, cw, cb, w_down):
    g = h @ w_gate
    ext = jnp.concatenate([prev, g], axis=1)
    a = jax.nn.silu(causal_dwconv(ext, cw, cb)) * (h @ w_up)
    return a @ w_down, ext[:, ext.shape[1] - (FFN_CONV_W - 1):]

def decoder_layer(x, q_pos, lw, mem=None, past=None, page_table=None):
    (norm_mix_g, w_in, b_gate, cmp_k_pe, cmp_k_w1, cmp_k_b1, cmp_k_w2,
     cmp_v_pe, cmp_v_w1, cmp_v_b1, cmp_v_w2, conv_w, conv_b, conv_ln_g, conv_ln_b,
     grp_norm_attn_g, grp_norm_conv_g, w_out, norm_mem_g, mem_norm_g, w_mq, w_mk, w_mv, w_mo,
     norm_ffn_g, w_ffn_gate, w_ffn_up, ffn_conv_w, ffn_conv_b, w_ffn_down) = lw
    B, T, _ = x.shape
    h = rmsnorm(x, norm_mix_g)
    q, kc, vc, ks, vs, kw, vw, gates, glu = project(h, w_in, b_gate)

    if past is None:
        kc_all, vc_all, ks_all, vs_all = kc, vc, ks, vs
        conv_prev = jnp.zeros((B, CONV_W - 1, CONV_CH), x.dtype)
        ffn_prev = jnp.zeros((B, FFN_CONV_W - 1, D_FF), x.dtype)
        mk, mv = memory_kv(mem, mem_norm_g, w_mk, w_mv)
    else:
        (pool_kc, pool_vc, pool_ks, pool_vs, buf_kw, buf_vw, conv_prev, ffn_prev, mk, mv) = past

        def with_past(pool, new):
            old = pool[page_table].reshape(B, -1, N_KV_HEADS, HEAD_DIM)
            return jnp.concatenate([old, new], axis=1)

        kc_all, vc_all = with_past(pool_kc, kc), with_past(pool_vc, vc)
        ks_all, vs_all = with_past(pool_ks, ks), with_past(pool_vs, vs)

    L = kc_all.shape[1]
    kcc = compress(kc_all, cmp_k_pe, cmp_k_w1, cmp_k_b1, cmp_k_w2)
    vcc = compress(vc_all, cmp_v_pe, cmp_v_w1, cmp_v_b1, cmp_v_w2)
    n_sel = -(-L // SEL_BLOCK)
    kb, vb = to_blocks(ks_all, n_sel), to_blocks(vs_all, n_sel)

    if past is None:
        nb = T // Q_BLOCK
        qb = jnp.moveaxis(q.reshape(B, N_KV_HEADS, GQA, nb, Q_BLOCK, HEAD_DIM), 3, 0)
        o_c, o_s = lax.map(lambda blk: cmp_and_select(blk[0], blk[1], kcc, vcc, kb, vb),
                           (qb, q_pos.reshape(nb, Q_BLOCK)))
        unblock = lambda o: jnp.moveaxis(o, 0, 3).reshape(B, N_KV_HEADS, GQA, T, HEAD_DIM)
        o_c, o_s = unblock(o_c), unblock(o_s)
        o_w = banded_window_attention(q, kw, vw)
        w_p = min(WINDOW, T)
        new_kw, new_vw = kw[:, T - w_p:], vw[:, T - w_p:]
    else:
        o_c, o_s = cmp_and_select(q, q_pos, kcc, vcc, kb, vb)
        n_buf = buf_kw.shape[1]
        k_all = jnp.concatenate([buf_kw, kw], axis=1)
        v_all = jnp.concatenate([buf_vw, vw], axis=1)
        k_pos = q_pos[0] - n_buf + jnp.arange(n_buf + T)
        o_w = window_attention(q[:, :, :, None], q_pos[None], k_all[:, None], v_all[:, None], k_pos[None])[:, :, :, 0]
        new_kw, new_vw = k_all[:, T:], v_all[:, T:]

    o_attn = gates[..., 0:1] * o_c + gates[..., 1:2] * o_s + gates[..., 2:3] * o_w
    o_attn = o_attn.transpose(0, 3, 1, 2, 4).reshape(B, T, ATTN_W)
    o_conv, new_conv = conformer_conv(glu, conv_prev, conv_w, conv_b, conv_ln_g, conv_ln_b)
    mixed = jnp.concatenate([rmsnorm(o_attn, grp_norm_attn_g), rmsnorm(o_conv, grp_norm_conv_g)], axis=-1)
    x = x + mixed @ w_out
    x = x + memory_attention(rmsnorm(x, norm_mem_g), mk, mv, w_mq, w_mo)
    f, new_ffn = conv_ffn(rmsnorm(x, norm_ffn_g), ffn_prev, w_ffn_gate, w_ffn_up, ffn_conv_w, ffn_conv_b, w_ffn_down)
    x = x + f
    if past is None:
        return x, (kc, vc, ks, vs, new_kw, new_vw, new_conv, new_ffn, mk, mv)
    return x, (kc, vc, ks, vs, new_kw, new_vw, new_conv, new_ffn)

def setup_inputs(seed: int = 0) -> dict:
    key = jax.random.key(seed)
    keys = jax.random.split(key, 80)
    kit = iter(range(80))

    def nrm(shape, scale=1.0):
        return jax.random.normal(keys[next(kit)], shape, jnp.float32) * scale

    def gain(shape):
        return 1.0 + nrm(shape, 0.02)

    n_pages = PAST_LEN // PAGE_SIZE
    n_phys = (DEC_BATCH * n_pages * 5) // 4
    win_buf = min(WINDOW, PAST_LEN)
    page_table = jax.random.permutation(keys[next(kit)], n_phys)[:DEC_BATCH * n_pages]
    page_table = page_table.reshape(DEC_BATCH, n_pages).astype(jnp.int32)
    kv_pool = (DEPTH, n_phys, PAGE_SIZE, N_KV_HEADS, HEAD_DIM)
    win_shape = (DEPTH, DEC_BATCH, win_buf, N_KV_HEADS, HEAD_DIM)
    mem_shape = (DEPTH, DEC_BATCH, N_MEM, MEM_HEADS, MEM_HEAD_DIM)
    return {
        'x_prompt': nrm((BATCH, SEQ, D_MODEL)),
        'x_sample': nrm((DEC_BATCH, DEC_SEQ, D_MODEL)),
        'cache_k_cmp': nrm(kv_pool),
        'cache_v_cmp': nrm(kv_pool),
        'cache_k_sel': nrm(kv_pool),
        'cache_v_sel': nrm(kv_pool),
        'cache_k_win': nrm(win_shape),
        'cache_v_win': nrm(win_shape),
        'state_conv': nrm((DEPTH, DEC_BATCH, CONV_W - 1, CONV_CH), 0.5),
        'state_ffn_conv': nrm((DEPTH, DEC_BATCH, FFN_CONV_W - 1, D_FF)),
        'cache_mem_k': nrm(mem_shape),
        'cache_mem_v': nrm(mem_shape),
        'page_table': page_table,
        'mem_prompt': nrm((BATCH, N_MEM, D_MODEL)),
        'norm_mix_g': gain((DEPTH, D_MODEL)),
        'w_in': nrm((DEPTH, D_MODEL, IN_COLS), D_MODEL ** -0.5),
        'b_gate': nrm((DEPTH, GATE_COLS), 0.1),
        'cmp_k_pe': nrm((DEPTH, BLOCK_CMP, HEAD_DIM), 0.5),
        'cmp_k_w1': nrm((DEPTH, BLOCK_CMP * HEAD_DIM, CMP_HID), (BLOCK_CMP * HEAD_DIM) ** -0.5),
        'cmp_k_b1': nrm((DEPTH, CMP_HID), 0.02),
        'cmp_k_w2': nrm((DEPTH, CMP_HID, HEAD_DIM), CMP_HID ** -0.5),
        'cmp_v_pe': nrm((DEPTH, BLOCK_CMP, HEAD_DIM), 0.5),
        'cmp_v_w1': nrm((DEPTH, BLOCK_CMP * HEAD_DIM, CMP_HID), (BLOCK_CMP * HEAD_DIM) ** -0.5),
        'cmp_v_b1': nrm((DEPTH, CMP_HID), 0.02),
        'cmp_v_w2': nrm((DEPTH, CMP_HID, HEAD_DIM), CMP_HID ** -0.5),
        'conv_w': nrm((DEPTH, CONV_W, CONV_CH), CONV_W ** -0.5),
        'conv_b': nrm((DEPTH, CONV_CH), 0.02),
        'conv_ln_g': gain((DEPTH, CONV_CH)),
        'conv_ln_b': nrm((DEPTH, CONV_CH), 0.02),
        'grp_norm_attn_g': gain((DEPTH, ATTN_W)),
        'grp_norm_conv_g': gain((DEPTH, CONV_CH)),
        'w_out': nrm((DEPTH, D_MODEL, D_MODEL), D_MODEL ** -0.5),
        'norm_mem_g': gain((DEPTH, D_MODEL)),
        'mem_norm_g': gain((DEPTH, D_MODEL)),
        'w_mq': nrm((DEPTH, D_MODEL, MEM_W), D_MODEL ** -0.5),
        'w_mk': nrm((DEPTH, D_MODEL, MEM_W), D_MODEL ** -0.5),
        'w_mv': nrm((DEPTH, D_MODEL, MEM_W), D_MODEL ** -0.5),
        'w_mo': nrm((DEPTH, MEM_W, D_MODEL), MEM_W ** -0.5),
        'norm_ffn_g': gain((DEPTH, D_MODEL)),
        'w_ffn_gate': nrm((DEPTH, D_MODEL, D_FF), D_MODEL ** -0.5),
        'w_ffn_up': nrm((DEPTH, D_MODEL, D_FF), D_MODEL ** -0.5),
        'ffn_conv_w': nrm((DEPTH, FFN_CONV_W, D_FF), FFN_CONV_W ** -0.5),
        'ffn_conv_b': nrm((DEPTH, D_FF), 0.02),
        'w_ffn_down': nrm((DEPTH, D_FF, D_MODEL), D_FF ** -0.5),
        'norm_final_g': gain((D_MODEL,)),
    }

def reference(x_prompt, x_sample, cache_k_cmp, cache_v_cmp, cache_k_sel, cache_v_sel, cache_k_win, cache_v_win,
              state_conv, state_ffn_conv, cache_mem_k, cache_mem_v, page_table, mem_prompt,
              norm_mix_g, w_in, b_gate, cmp_k_pe, cmp_k_w1, cmp_k_b1, cmp_k_w2, cmp_v_pe, cmp_v_w1, cmp_v_b1, cmp_v_w2,
              conv_w, conv_b, conv_ln_g, conv_ln_b, grp_norm_attn_g, grp_norm_conv_g, w_out,
              norm_mem_g, mem_norm_g, w_mq, w_mk, w_mv, w_mo,
              norm_ffn_g, w_ffn_gate, w_ffn_up, ffn_conv_w, ffn_conv_b, w_ffn_down, norm_final_g):
    weights = (norm_mix_g, w_in, b_gate, cmp_k_pe, cmp_k_w1, cmp_k_b1, cmp_k_w2,
               cmp_v_pe, cmp_v_w1, cmp_v_b1, cmp_v_w2, conv_w, conv_b, conv_ln_g, conv_ln_b,
               grp_norm_attn_g, grp_norm_conv_g, w_out, norm_mem_g, mem_norm_g, w_mq, w_mk, w_mv, w_mo,
               norm_ffn_g, w_ffn_gate, w_ffn_up, ffn_conv_w, ffn_conv_b, w_ffn_down)
    past_len = page_table.shape[1] * PAGE_SIZE
    pos_p = jnp.arange(x_prompt.shape[1])
    pos_s = past_len + jnp.arange(x_sample.shape[1])
    xp, xs = x_prompt, x_sample
    st_p, st_s = [], []
    for l in range(DEPTH):
        lw = tuple(w[l] for w in weights)
        xp, sp = decoder_layer(xp, pos_p, lw, mem=mem_prompt)
        past = (cache_k_cmp[l], cache_v_cmp[l], cache_k_sel[l], cache_v_sel[l], cache_k_win[l], cache_v_win[l],
                state_conv[l], state_ffn_conv[l], cache_mem_k[l], cache_mem_v[l])
        xs, ss = decoder_layer(xs, pos_s, lw, past=past, page_table=page_table)
        st_p.append(sp)
        st_s.append(ss)
    stk = lambda sts, i: jnp.stack([s[i] for s in sts])
    y_prompt = rmsnorm(xp, norm_final_g)
    y_sample = rmsnorm(xs, norm_final_g)
    return (y_prompt, y_sample,
            stk(st_p, 0), stk(st_p, 1), stk(st_p, 2), stk(st_p, 3), stk(st_p, 4), stk(st_p, 5),
            stk(st_p, 6), stk(st_p, 7), stk(st_p, 8), stk(st_p, 9),
            stk(st_s, 0), stk(st_s, 1), stk(st_s, 2), stk(st_s, 3), stk(st_s, 4), stk(st_s, 5),
            stk(st_s, 6), stk(st_s, 7))


_drawn_inputs = setup_inputs


def setup_inputs(seed=0):
    import zlib

    import numpy as np

    out = dict(_drawn_inputs(seed))
    spreads = {}
    factors = {'b_gate': 2.915,
     'cmp_k_b1': 8.0,
     'cmp_v_b1': 4.022,
     'conv_ln_g': 4.873,
     'conv_ln_b': 5.004,
     'grp_norm_attn_g': 5.264,
     'grp_norm_conv_g': 5.118,
     'norm_mem_g': 8.0,
     'mem_norm_g': 2.843,
     'norm_ffn_g': 8.12,
     'ffn_conv_b': 7.212,
     'norm_final_g': 8.219}
    for name, (base, spread) in spreads.items():
        noise = np.random.default_rng([zlib.crc32(name.encode()), seed]).standard_normal(out[name].shape)
        drawn = base * np.exp(spread * noise) if base else spread * noise
        out[name] = __import__('jax').numpy.asarray(drawn.astype(out[name].dtype))
    for name, factor in factors.items():
        out[name] = (out[name] * factor).astype(out[name].dtype)
    return out
```

```python
from contextlib import ExitStack

import numpy as np

import concourse.bass as bass
from concourse import mybir

F32 = mybir.dt.float32
I32 = mybir.dt.int32
ALU = mybir.AluOpType
ACT = mybir.ActivationFunctionType
AX_X = mybir.AxisListType.X
ds = bass.ds

P = 128
D = 2048
KT = D // P
SEQ = 512
NB, NT = 8, 4
SAMP = NB * NT
TOK = SEQ + SAMP
HALF = TOK // 2
QB = SEQ // P
HEADS, KV, GQA, DH = 8, 2, 4, 128
ATT = HEADS * DH
KVW = KV * DH
GATES = 3 * HEADS
CCH = D - ATT
CT = CCH // P
CW = 31
PREV = CW - 1
FF = 5632
FT = FF // P
FW = 3
NMEM, MH = 256, 4
MEMW = MH * DH
PAST, PAGE = 1024, 128
PAGES = PAST // PAGE
BLK, STR, HID = 32, 16, 256
HT = HID // P
CHUNKS = PAST // STR
NC_S = CHUNKS - 1
NC_P = SEQ // STR - 1
SEL = 64
N_SEL = -(-(PAST + NT) // SEL)
WIN = 512
SCALE = DH ** -0.5
EPS = 1e-6
NEG = -1e30
FLOOR = -1e25
SEG = 4 * KV
T_Q, T_KC, T_VC, T_KS, T_VS, T_KW, T_VW = 0, 8, 10, 12, 14, 16, 18
N_QKV = 20
G_COL = ATT + 6 * KVW
GLU = G_COL + GATES
FFN_CHUNKS = [12, 12, 10, 10]


def constants():
    q = np.arange(P)
    parts = {}
    parts["ident"] = np.eye(P)
    b, t = q // 16, q % 4
    winhead = np.where(np.arange(4)[None, :] <= t[:, None], NEG, 0.0)
    zeros = np.zeros((P, 508))
    diag = np.where(q[None, :] <= q[:, None], 0.0, NEG)
    parts["mask"] = np.concatenate([winhead, zeros, diag], 1)
    end = np.arange(NC_P) * STR + BLK - 1
    parts["cmask"] = np.concatenate([np.where(end[None, :] <= (qb * P + q)[:, None], 0.0, NEG) for qb in range(QB)], 1)
    c = np.arange(SAMP)
    parts["nmask"] = np.where((c[None, :] // NT == b[:, None]) & (c[None, :] % NT <= t[:, None]), 0.0, NEG)
    parts["jidx"] = np.tile(np.arange(1, N_SEL - 2), (P, 1))
    parts["group"] = (b[:, None] == b[None, :]) & (t[:, None] == t[None, :])
    i, j = np.arange(P)[:, None] * STR, np.arange(N_SEL)[None, :] * SEL
    parts["overlap"] = np.clip(np.minimum(i + BLK, j + SEL) - np.maximum(i, j), 0, None) / BLK
    parts["eps"] = np.full((P, 1), EPS)
    at, cols = {}, 0
    for n, a in parts.items():
        at[n] = (cols, cols + a.shape[1])
        cols += a.shape[1]
    sel = np.zeros((SAMP, GQA, P))
    for r in range(P):
        sel[(r // 16) * NT + r % 4, (r // 4) % 4, r] = 1.0
    return np.concatenate(list(parts.values()), 1).astype(np.float32), at, sel.reshape(SAMP, GQA * P).astype(np.float32)


class Chain:

    def __init__(self, eng, sem, base=0):
        self.eng, self.sem, self.n = eng, sem, base

    def tick(self, ins):
        ins.then_inc(self.sem, 1)
        self.n = self.n + 1

    def wait(self):
        self.eng.wait_ge(self.sem, self.n)

    def step(self, ins):
        self.tick(ins)
        self.wait()


def hybrid_step(nc, A, O):
    _, CONST_AT, _ = constants()
    NCONST = max(b for _, b in CONST_AT.values())
    with ExitStack() as ctx:
        def sb(name, shape, dt=F32):
            return ctx.enter_context(nc.sbuf_tensor(name, shape, dt))

        def sem(name):
            return ctx.enter_context(nc.semaphore(name))

        XT = sb("xT", [P, KT, TOK])
        RB = sb("region_b", [P, KT * TOK])
        RC = sb("region_c", [P, N_QKV * TOK])
        RF = sb("region_f", [P, KT * TOK])
        RING = sb("weight_ring", [P, 4, 2048])
        VT = sb("v_tok", [P, 5, 4, DH])
        CST = sb("consts", [P, NCONST])
        ONES = sb("ones", [P, P])
        CONVP = sb("convp", [P, CT, 35])
        VEC = sb("vecs", [P, KT, 6])
        CMPP = sb("cmpp", [P, 68])
        GTOK = sb("gate_tok", [P, 5, GATES])
        GSMP = sb("gate_sample", [P, KV, 3])
        W2 = sb("cmp_w2", [P, 2, HT, DH])
        RS = sb("rstd", [P, TOK])
        SG = sb("scratch", [P, TOK])
        EX = sb("ext", [P, 2, SEQ + PREV + NB * (PREV + NT)])
        BG = sb("b_gate_col", [GATES, 1])
        STATS = sb("stats", [P, 200])
        BIAS = sb("cmp_bias", [P, HT])
        CWT = sb("tile_taps", [P, 2, 35])
        PTB = sb("page_table", [1, NB * PAGES], I32)
        PS = ctx.enter_context(nc.psum_tensor("ps", [P, 8, 512], F32))

        def cst(name, rows=P):
            a, b = CONST_AT[name]
            return CST[0:rows, a:b]

        IDENT = cst("ident")

        cursor = [0]

        def stat(*shape):
            n = int(np.prod(shape))
            cursor[0] += n
            return flat(STATS, cursor[0] - n, *shape)

        def flat(t, off, *shape, rows=P):
            n = int(np.prod(shape))
            v = t[0:rows, off:off + n]
            names = "abcd"[:len(shape)]
            if len(shape) == 1:
                return v
            return v.rearrange(f"p ({' '.join(names)}) -> p {' '.join(names)}", **dict(zip(names, shape)))

        def ring(k, *shape):
            return flat(RING[:, :, :].rearrange("p a b -> p (a b)"), k, *shape)

        def halves(ap):
            return ap.rearrange("p (h t) -> p h t", h=2)

        HTL = flat(RB, 0, KT, TOK)
        C = flat(RC, 0, N_QKV, TOK)
        MIX = flat(RF, 0, KT, TOK)
        PAIR = [PS[:, 2 * j:2 * j + 2, 0:HALF] for j in range(4)]
        PSX = PS[:, :, :].rearrange("p b c -> p (b c)")

        X4 = [flat(RB, tt * D, D) for tt in range(4)]
        XS = flat(RC, 0, D, rows=SAMP)
        VECR = flat(RC, D, D, rows=6)
        CONVR = flat(RC, 2 * D, CCH, rows=35)
        CMPR = flat(RC, 2 * D + CCH, DH, rows=68)
        STR_ = flat(RC, 2 * D + CCH + DH, 2, CCH, rows=120)
        STT = flat(RF, 0, CT, NB * PREV)
        UC = flat(RF, 1920, CT, PREV + SAMP)
        PROD = flat(RF, 1920 + CT * (PREV + SAMP), NB, NT, CW)
        SELG = flat(RF, 3408, GQA, P, rows=SAMP)
        WG = flat(RF, 8 * TOK - KT * GATES, KT, GATES)
        GT = flat(VT[:, :, :, :].rearrange("p a b c -> p (a b c)"), 0, TOK, rows=GATES)
        TOKM = flat(RB, 0, 5, 12, DH)
        KX = flat(RB, 0, STR, SEG, CHUNKS)
        KP = flat(EX[:, :, :].rearrange("p a b -> p (a b)"), 0, STR, 3, SEQ // STR)
        HIDS = flat(RC, T_VS * TOK, HT, SEG * NC_S)
        HIDP = flat(SG, 0, HT, KV * NC_P)
        KC = flat(RC, T_VW * TOK, 2 * SEG * NC_S + KV * NC_P)
        VC = flat(RF, 0, 2 * SEG, DH)
        VCP = flat(RF, 2048, KV, DH)
        PGS = [flat(RF, 2304 + 1024 * s, 4, KVW) for s in range(2)]
        assert 2304 + 2048 <= 8 * TOK and 3408 + 512 + KT * GATES <= 8 * TOK

        s_const = sem("const_loaded")
        s_ones = sem("ones_set")
        s_x = [sem(f"x_loaded{t}") for t in range(5)]
        s_rows = sem("rows_loaded")
        s_wg = sem("gate_weights_loaded")
        s_slab = [sem(f"slab_loaded{j}") for j in range(4)]
        s_used = [sem(f"slab_used{j}") for j in range(4)]
        s_ps = [sem(f"psum_pair_read{j}") for j in range(4)]
        s_tr = sem("transposed")
        s_te = [sem("turned_by_act"), sem("turned_by_dve")]
        s_sq = sem("squares_ready")
        s_ss = sem("squares_summed")
        s_rt = sem("root_ready")
        s_rs = sem("rstd_ready")
        s_h = sem("normed_ready")
        s_ad = sem("act_own")
        s_dv = sem("dve_own")
        s_gm = sem("gate_product")
        s_gs = sem("gate_sigmoid")
        s_sg = sem("glu_sigmoid")
        s_u = sem("glu_gated")
        s_cv = sem("conv_tile_done")
        s_cvl = sem("conv_own")
        s_mu = sem("ln_centered")
        s_yl = sem("ln_scaled")
        s_y = sem("conv_silu")
        s_tok = sem("kv_rows_stored")
        s_spread = sem("gates_spread")
        s_out = sem("stored")
        s_pool = sem("pool_own")

        jobs, total = {}, 0
        for name, n in (("x", 20), ("vec", 1), ("conv", 1), ("state", 4), ("cmpp", 1),
                        ("gate", 1), ("kvtok", 15), ("ucap", 4), ("pages", 64), ("attn", 48),
                        ("s_cmp", 4), ("s_win", 2 * NB), ("s_sel", 4 * NB), ("s_p", 8),
                        ("memr", 8), ("memk", 2), ("mp", 8), ("ms", 2 * NB), ("msp", 1),
                        ("ffp", 2), ("ffs", 11), ("y", 20)):
            jobs[name] = total
            total += n

        def end_of(name):
            names = list(jobs)
            k = names.index(name)
            return jobs[names[k + 1]] if k + 1 < len(names) else total

        def turned(eng, upto):
            for p in range(2):
                if (upto + 1 - p) // 2:
                    eng.wait_ge(s_te[p], (upto + 1 - p) // 2)

        SGR = {"glu": 0, "qkv": 4, "w1k": 9, "w1v": 10, "out": 11, "mk": 15, "mv": 16, "mq": 17, "mo": 18, "ffn": 19}
        PGR = {"glu": 0, "qkv": 4, "out": 9, "mq": 13, "mo": 14, "ffn": 18}
        ffn_plan, g, f0 = [], 0, 0
        for n in FFN_CHUNKS:
            ffn_plan.append((f0, n, g, g + n // 2))
            g += n // 2 + 4
            f0 += n
        NRM, c = {}, 0
        for k, (name, n) in enumerate((("mix", 16), ("lnmu", 8), ("lnvar", 8), ("gconv", 8), ("gattn", 8),
                                       ("mem", 16), ("ffn", 16), ("final", 16))):
            NRM[name] = (k, c, n)
            c += n
        ROOTS = {n: k - (k > 1) for n, (k, _, _) in NRM.items()}
        HBASE, c = {}, 0
        for name, n in (("mix", 16), ("gconv", 8), ("gattn", 8), ("mem", 16), ("ffn", 16), ("final", 16)):
            HBASE[name] = c
            c += n

        N_TOK = 6 + 4 + 2 * NB + 1 + NB
        SQ = [EX[:, k, 0:TOK] for k in range(2)]

        def bank(k):
            return PS[:, 6 + k % 2, :]

        def x_job(k):
            tt, m = divmod(k - jobs["x"], 4)
            n = P if tt < 4 else SAMP
            return [(XT[:, 4 * m:4 * m + 4, tt * P:tt * P + n],
                     bank(k).rearrange("p (a t) -> p a t", a=4)[:, :, 0:n])]

        def vec_job(k):
            return [(VEC[:, :, :].rearrange("p a b -> p (a b)"), bank(k)[:, 0:KT * 6])]

        def conv_job(k):
            return [(CONVP[:, :, :].rearrange("p a b -> p (a b)"), bank(k)[:, 0:CT * 35])]

        def state_job(k):
            m = k - jobs["state"]
            return [(STT[:, 2 * m:2 * m + 2, :], bank(k)[:, 0:480].rearrange("p (a t) -> p a t", a=2))]

        def cmpp_job(k):
            return [(CMPP[:, :], bank(k)[:, 0:68])]

        def kvtok_job(k):
            tt, m = divmod(k - jobs["kvtok"], 3)
            n = P if tt < 4 else SAMP
            src = bank(k).rearrange("p (a d) -> p a d", a=4)
            out = [(TOKM[0:n, tt, 4 * m:4 * m + 4, :], src[0:n])]
            if m:
                out.append((VT[0:n, tt, 2 * m - 2:2 * m, :], src[0:n, 2:4]))
            return out

        def gate_job(k):
            return [(GTOK[:, 0:4, :], bank(k)[:, 0:96].rearrange("p (a g) -> p a g", a=4)),
                    (GTOK[0:SAMP, 4, :], bank(k)[0:SAMP, 96:120])]

        UR = [flat(RB, 7680, CCH), flat(RC, T_VS * TOK, CCH)]

        def ucap_job(k):
            which, m = divmod(k - jobs["ucap"], 2)
            n = PREV if which == 0 else SAMP
            return [(UR[which][0:n, m * 512:m * 512 + 512], bank(k)[0:n, :])]

        def pages_job(k):
            r, kv = divmod(k - jobs["pages"], 2)
            p_, r = divmod(r, 8)
            b, pg4 = divmod(r, 2)
            dst = KX[:, :, b * KV + kv, pg4 * 32:pg4 * 32 + 32]
            return [(dst, bank(k).rearrange("p (c l) -> p l c", l=STR))]

        PBUF = [flat(RB, 4352 * s, GQA, 1055) for s in range(2)]
        PT_ = [ring(512 * s, 512) for s in range(9)]
        UNITS = [(kv, qb) for kv in range(KV) for qb in range(QB)]
        UJOB = []
        c = jobs["attn"]
        for kv, qb in UNITS:
            UJOB.append(c)
            c += 2 * (qb + 1) + 1

        def attn_pieces(u):
            kv, qb = UNITS[u]
            out = [(j * P, P, VT[:, j, 2 + kv, :]) for j in range(qb + 1)]
            out += [(512 + j * P, P, VT[:, j, kv, :]) for j in range(qb + 1)]
            return out + [(1024, NC_P, VCP[0:NC_P, kv, :])]

        def attn_job(k):
            u = max(i for i in range(8) if UJOB[i] <= k)
            n = attn_pieces(u)[k - UJOB[u]][1]
            return [(PT_[k - UJOB[u]][0:n, :], bank(k)[0:n, :])]

        s_sc = sem("scores")
        s_scr = sem("scores_read")
        s_csc = sem("cmp_scores")
        s_ccr = sem("cmp_scores_read")
        s_nm = sem("neg_max")
        s_ex = sem("exps")
        s_pn = sem("probs_scaled")
        s_pv = sem("values_summed")
        s_ov = sem("attention_stored")
        s_w2 = sem("w2_loaded")
        s_kp = sem("prompt_rows_ready")
        s_cp = sem("cmp_prompt_product")
        s_cb = sem("cmp_bias_ready")
        s_cg = sem("cmp_product")
        s_ge = sem("cmp_gelu")
        s_cw = sem("cmp_out")
        s_cwr = sem("cmp_out_read")
        s_pg = [sem(f"pages_loaded{k}") for k in range(2)]
        s_ptb = sem("page_table_loaded")

        QA = flat(RB, 0, KV, P)
        QP = flat(RB, 256, KV, NB, P)
        KTS = [flat(RB, 2304 + 2048 * s, 2048) for s in range(1)]
        PSS = flat(RB, 4352, KV, 1056)
        PSW = flat(RB, 6464, KV, 544)
        PSC = flat(RB, 7552, KV, 2, NC_S)
        PTS = ring(4096, KV, 15, P)
        PCT = flat(RB, 7808, KV, P)
        IMP = flat(RB, 8064, KV, N_SEL)
        PEN = flat(RB, 8100, KV, 16)
        SEQL = flat(RB, 8140, KV, 2, 14)
        SRAW = [ring(2048 * s, 2048) for s in range(2)]
        WRAW = [ring(2048 * s, 4, KVW) for s in range(2)]
        s_sraw = [sem(f"sample_rows_loaded{k}") for k in range(2)]
        s_sus = sem("sample_rows_used")
        s_q = sem("sample_q_placed")
        s_s1 = sem("sample_first_scores")
        s_sw = sem("sample_key_scores")
        s_kt = sem("sample_keys_used")
        s_ss_ = sem("sample_softmax")
        s_se = sem("sample_exps")
        s_im = sem("importance")
        s_imr = sem("importance_read")
        s_so = sem("sample_values_summed")
        s_sor = sem("sample_out_stored")
        MR = [flat(RB, 2048 * s, D) for s in range(2)]
        MSCR = flat(RB, 4096, D)
        MT = flat(RC, 0, KT, NMEM)
        KMT = flat(RC, 4096, 2, MEMW)
        VMT = flat(RC, 5120, 2, MEMW)
        KMD = flat(RC, 6144, MH, NMEM)
        QM = flat(RC, 7168, MH, TOK)
        PMB = [flat(RF, 1024 * s, MH, NMEM) for s in range(2)]
        PMT = [flat(RF, 2048 + 512 * s, 2, 2, P) for s in range(2)]
        QMP = flat(RF, 3072, MH, NB, SAMP)
        PMS = flat(RF, 4096, NMEM)
        PMST = flat(RF, 4352, 2, P)
        KMR = [flat(RB, 1024 * s, 2, MEMW) for s in range(2)]
        KMS = [flat(RB, 2048 + 1024 * s, MH, NMEM) for s in range(2)]
        VMR = [flat(RB, 4096 + 1024 * s, 2, MEMW) for s in range(2)]
        s_mr = sem("memory_rows")
        s_msum = sem("memory_sums")
        s_mn = sem("memory_normed")
        s_mkv = sem("memory_kv_product")
        s_mke = sem("memory_kv_read")
        s_msc = sem("memory_scores")
        s_mnm = sem("memory_neg_max")
        s_mex = sem("memory_exps")
        s_mpn = sem("memory_probs")
        s_mpv = sem("memory_values")
        s_mov = sem("memory_out")
        s_qmp = sem("memory_q_placed")
        s_mop = sem("memory_out_product")
        s_mrt = sem("memory_root")
        s_smx = sem("sample_neg_max")
        s_kmr = [sem(f"memory_key_rows{k}") for k in range(2)]
        s_vmr = [sem(f"memory_value_rows{k}") for k in range(2)]
        AT = flat(RC, 0, 12, TOK)
        FP = flat(RC, 6528, FT, 20)
        GX = [flat(RC, 7408 + 562 * s, 2 + SEQ + NB * 6) for s in range(2)]
        FC = [flat(RC, 8532 + TOK * s, TOK) for s in range(2)]
        GSV = flat(RC, 9620, FT, 18)
        MX, NM, SUM, FAC = stat(2, 12), stat(2, 12), stat(2, 12), stat(2, 12)
        SMC, SMS, SMW = stat(KV), stat(KV, 3), stat(KV, 2)
        SNM, SSM, SFC = stat(6), stat(6), stat(6)
        SMN, SJM = stat(KV), stat(KV)
        MSQ, MRT, MRI = stat(2), stat(2), stat(2)
        MMX, MNM, MSU, MFC = stat(2, MH), stat(2, MH), stat(2, MH), stat(2, MH)
        FWT = [EX[:, s, 0:20] for s in range(2)]
        FR = flat(RF, 0, FF, rows=20)
        FSR = flat(RF, 0, FF, rows=18)
        s_fr = sem("ffn_rows_loaded")
        s_gx = sem("ffn_gate_copied")
        s_fc = sem("ffn_conv")
        s_fs = sem("ffn_silu")
        s_fl = sem("ffn_own")
        YR = [flat(RC, 2048 * s, D) for s in range(5)]

        def mem_job(k):
            if k < end_of("memr"):
                tt, m = divmod(k - jobs["memr"], 4)
                return [(MT[:, 4 * m:4 * m + 4, tt * P:(tt + 1) * P], bank(k).rearrange("p (a t) -> p a t", a=4))]
            if k < end_of("memk"):
                tt = k - jobs["memk"]
                return [(KMD[:, :, tt * P:(tt + 1) * P], bank(k).rearrange("p (a t) -> p a t", a=4))]
            if k < end_of("mp"):
                s = k - jobs["mp"]
                return [(PMT[s % 2].rearrange("p a b c -> p (a b c)"), bank(k))]
            if k < end_of("ms"):
                b, tt = divmod(k - jobs["ms"], 2)
                return [(KMS[b % 2][:, :, tt * P:(tt + 1) * P], bank(k).rearrange("p (a t) -> p a t", a=4))]
            return [(PMST.rearrange("p a b -> p (a b)"), bank(k)[:, 0:256])]

        def s_job(k):
            if k < end_of("s_cmp"):
                kv, gated = divmod(k - jobs["s_cmp"], 2)
                dst = PTS[0:NC_S, kv, 14, :] if gated else PCT[0:NC_S, kv, :]
                return [(dst, bank(k)[0:NC_S, 0:P])]
            if k < end_of("s_win"):
                b, kv = divmod(k - jobs["s_win"], 2)
                return [(KTS[0].rearrange("p (s k t) -> p s k t", s=2, k=2)[:, b % 2, kv, :], bank(k))]
            if k < end_of("s_sel"):
                r, h = divmod(k - jobs["s_sel"], 2)
                kv = r % 2
                return [(KTS[0].rearrange("p (k h t) -> p k h t", k=2, h=2)[:, kv, h, :], bank(k))]
            kv, m = divmod(k - jobs["s_p"], 4)
            dst = PTS[:, kv, 4 * m:4 * m + 4, :] if m < 2 else None
            src = bank(k).rearrange("p (a r) -> p a r", a=4)
            if m == 3:
                return [(PTS[0:SAMP, kv, 8, :], src[0:SAMP, 0]), (PTS[0:SAMP, kv, 13, :], src[0:SAMP, 1])]
            if m == 2:
                dst = PTS[:, kv, 9:13, :]
            return [(dst, src)]

        def ffs_job(k):
            m = k - jobs["ffs"]
            return [(FSR[:, m * 512:(m + 1) * 512], bank(k)[0:18, :])]

        def ffp_job(k):
            m = k - jobs["ffp"]
            return [(FP[:, 22 * m:22 * m + 22, :].rearrange("p a b -> p (a b)"), bank(k)[:, 0:440])]

        def y_job(k):
            tt, m = divmod(k - jobs["y"], 4)
            n = P if tt < 4 else SAMP
            return [(YR[tt][0:n, m * 512:(m + 1) * 512], bank(k)[0:n, :])]

        w_in, w_out = A["w_in"][0], A["w_out"][0]

        def w_tiles(w):
            return w.rearrange("(t p) n -> p t n", p=P)

        def steps(eng, n, body, peel=False):
            if peel:
                body(0)
            with eng.Fori(int(peel), n) as i:
                body(i)

        block = ctx.enter_context(nc.Block())

        @block.sync
        def _(sp):
            sp.dma_start(CST[:, :], A["consts"]).then_inc(s_const, 16)
            for tt in range(4):
                sp.dma_start(X4[tt], A["x_prompt"][0, tt * P:(tt + 1) * P, :]).then_inc(s_x[tt], 16)
            sp.dma_start(XS, A["x_sample"].rearrange("b t d -> (b t) d")).then_inc(s_x[4], 16)
            for r, n in enumerate(("norm_mix_g", "norm_mem_g", "mem_norm_g", "norm_ffn_g")):
                sp.dma_start(VECR[r:r + 1, :], A[n]).then_inc(s_rows, 16)
            sp.dma_start(VECR[4:5, :], A["norm_final_g"].rearrange("(o d) -> o d", o=1)).then_inc(s_rows, 16)
            sp.dma_start(VECR[5:6, 0:ATT], A["grp_norm_attn_g"]).then_inc(s_rows, 16)
            sp.dma_start(VECR[5:6, ATT:D], A["grp_norm_conv_g"]).then_inc(s_rows, 16)
            sp.dma_start(CONVR[0:CW, :], A["conv_w"][0]).then_inc(s_rows, 16)
            for r, n in enumerate(("conv_b", "conv_ln_g", "conv_ln_b", "grp_norm_conv_g")):
                sp.dma_start(CONVR[CW + r:CW + r + 1, :], A[n]).then_inc(s_rows, 16)
            for k, kind in enumerate("kv"):
                sp.dma_start(CMPR[34 * k:34 * k + BLK, :], A[f"cmp_{kind}_pe"][0]).then_inc(s_rows, 16)
                sp.dma_start(CMPR[34 * k + BLK:34 * k + 34, :],
                             A[f"cmp_{kind}_b1"].rearrange("o (f p) -> (o f) p", p=P)).then_inc(s_rows, 16)
                sp.dma_start(W2[:, k, :, :], A[f"cmp_{kind}_w2"][0].rearrange("(f p) d -> p f d", p=P)).then_inc(s_w2, 16)
            for k in range(2):
                sp.dma_start(STR_[:, k, :], A["state_conv"][0, 4 * k:4 * k + 4].rearrange("b t c -> (b t) c")).then_inc(s_rows, 16)
            sp.dma_start(WG, w_tiles(w_in)[:, :, G_COL:G_COL + GATES]).then_inc(s_wg, 16)
            sp.dma_start(BG[:, :], A["b_gate"].rearrange("o g -> g o")).then_inc(s_wg, 16)
            sp.dma_start(SELG.rearrange("p a b -> p (a b)"), A["gate_rows"]).then_inc(s_wg, 16)
            sp.dma_start(PTB[:, :], A["page_table"].rearrange("b n -> (b n)").rearrange("(o n) -> o n", o=1)).then_inc(s_ptb, 16)

            def glu_slabs(i):
                for j in range(4):
                    if type(i) is not int:
                        sp.wait_ge(s_used[j], i + SGR["glu"])
                    col = i * 256 + (GLU + (j // 2) * P + (j % 2) * CCH)
                    sp.dma_start(RING[:, j, :].rearrange("p (t n) -> p t n", t=KT),
                                 w_tiles(w_in)[:, :, ds(col, P)]).then_inc(s_slab[j], 16)

            steps(sp, 4, glu_slabs, peel=True)
            with sp.Fori(0, 5) as i:
                for j in range(4):
                    sp.wait_ge(s_used[j], i + SGR["qkv"])
                    sp.dma_start(RING[:, j, :].rearrange("p (t n) -> p t n", t=KT),
                                 w_tiles(w_in)[:, :, ds(i * 512 + j * P, P)]).then_inc(s_slab[j], 16)

            sp.wait_ge(s_ptb, 16)
            turned(sp, end_of("ucap"))
            sp.wait_ge(s_cv, CT)
            sp.wait_ge(s_gm, 2)
            step = 0
            for p_ in range(4):
                kind, half = divmod(p_, 2)
                if half == 0:
                    for j in range(4):
                        sp.wait_ge(s_used[j], SGR["w1k"] + kind)
                        w1 = A[f"cmp_{'kv'[kind]}_w1"][0].rearrange("(l p) f -> p l f", p=P)
                        sp.dma_start(RING[:, j, :].rearrange("p (l f) -> p l f", l=8), w1[:, 8 * j:8 * j + 8, :]).then_inc(s_slab[j], 16)
                pool = A[f"cache_{'kv'[kind]}_cmp"][0]
                for b in range(4):
                    for pg4 in range(2):
                        if step >= 2:
                            sp.wait_ge(s_tr, jobs["pages"] + 2 * (step - 1))
                        for k in range(4):
                            at = (half * 4 + b) * PAGES + pg4 * 4 + k
                            page = sp.value_load(PTB[0:1, at:at + 1], min_val=0, max_val=79)
                            sp.dma_start(PGS[step % 2][:, k, :],
                                         pool[ds(page, 1)].rearrange("o t k d -> (o t) (k d)")).then_inc(s_pg[step % 2], 16)
                        step += 1

            sp.wait_ge(s_pv, 8)
            for b in range(NB):
                if b >= 2:
                    sp.wait_ge(s_tr, jobs["s_win"] + 2 * (b - 1))
                sp.dma_start(WRAW[b % 2], A["cache_k_win"][0, b].rearrange("(t p) k d -> p t (k d)", p=P)).then_inc(s_sraw[b % 2], 16)
            for b in range(NB):
                sp.wait_ge(s_tr, jobs["s_win"] + 2 * (NB - 1 + (b > 0)) if b < 2 else jobs["s_sel"] + 4 * (b - 1))
                for k in range(PAGES):
                    page = sp.value_load(PTB[0:1, b * PAGES + k:b * PAGES + k + 1], min_val=0, max_val=79)
                    sp.dma_start(SRAW[b % 2][:, k * KVW:(k + 1) * KVW],
                                 A["cache_k_sel"][0, ds(page, 1)].rearrange("o t k d -> (o t) (k d)")).then_inc(s_sraw[b % 2], 16)
            for b in range(NB):
                if b == 0:
                    sp.wait_ge(s_tr, end_of("s_sel"))
                else:
                    sp.wait_ge(s_so, b)
                for k in range(PAGES):
                    page = sp.value_load(PTB[0:1, b * PAGES + k:b * PAGES + k + 1], min_val=0, max_val=79)
                    sp.dma_start(SRAW[0][:, k * KVW:(k + 1) * KVW],
                                 A["cache_v_sel"][0, ds(page, 1)].rearrange("o t k d -> (o t) (k d)")).then_inc(s_sraw[0], 16)
                sp.dma_start(WRAW[1], A["cache_v_win"][0, b].rearrange("(t p) k d -> p t (k d)", p=P)).then_inc(s_sraw[1], 16)

            sp.wait_ge(s_sor, NB)
            for tt in range(2):
                sp.dma_start(MR[tt], A["mem_prompt"][0, tt * P:(tt + 1) * P, :]).then_inc(s_mr, 16)
            with sp.Fori(0, 4) as i:
                for j in range(4):
                    sp.wait_ge(s_used[j], i + SGR["out"])
                    sp.dma_start(RING[:, j, :].rearrange("p (t n) -> p t n", t=KT),
                                 w_tiles(w_out)[:, :, ds(i * 512 + j * P, P)]).then_inc(s_slab[j], 16)
            for k, n in enumerate(("w_mk", "w_mv")):
                for j in range(4):
                    sp.wait_ge(s_used[j], SGR["mk"] + k)
                    sp.dma_start(RING[:, j, :].rearrange("p (t n) -> p t n", t=4),
                                 w_tiles(A[n][0])[:, 4 * j:4 * j + 4, :]).then_inc(s_slab[j], 16)
            for j in range(4):
                sp.wait_ge(s_used[j], SGR["mq"])
                sp.dma_start(RING[:, j, :].rearrange("p (t n) -> p t n", t=KT),
                             w_tiles(A["w_mq"][0])[:, :, j * P:(j + 1) * P]).then_inc(s_slab[j], 16)
            for j in range(4):
                sp.wait_ge(s_used[j], SGR["mo"])
                sp.dma_start(RING[:, j, :].rearrange("p (t n) -> p t n", t=4),
                             w_tiles(A["w_mo"][0])[:, :, j * 512:(j + 1) * 512]).then_inc(s_slab[j], 16)
            for j in range(4):
                sp.wait_ge(s_used[j], SGR["mo"])
            for b in range(NB):
                if b >= 2:
                    sp.wait_ge(s_tr, jobs["ms"] + 2 * (b - 1))
                sp.dma_start(KMR[b % 2], A["cache_mem_k"][0, b].rearrange("(t p) h d -> p t (h d)", p=P)).then_inc(s_kmr[b % 2], 16)
            for b in range(NB):
                if b >= 2:
                    sp.wait_ge(s_mpv, QB + b - 1)
                sp.dma_start(VMR[b % 2], A["cache_mem_v"][0, b].rearrange("(t p) h d -> p t (h d)", p=P)).then_inc(s_vmr[b % 2], 16)
            sp.wait_ge(s_mov, QB + 1)
            sp.dma_start(FR[0:16, :], A["state_ffn_conv"][0].rearrange("b t c -> (b t) c")).then_inc(s_fr, 16)
            sp.dma_start(FR[16:19, :], A["ffn_conv_w"][0]).then_inc(s_fr, 16)
            sp.dma_start(FR[19:20, :], A["ffn_conv_b"]).then_inc(s_fr, 16)
            for f0, n, gu, gd in ffn_plan:
                with sp.Fori(0, n // 2) as i:
                    for j in range(4):
                        sp.wait_ge(s_used[j], i + (SGR["ffn"] + gu))
                        w = A["w_ffn_gate" if j % 2 == 0 else "w_ffn_up"][0]
                        sp.dma_start(RING[:, j, :].rearrange("p (t n) -> p t n", t=KT),
                                     w_tiles(w)[:, :, ds(i * 256 + (f0 + j // 2) * P, P)]).then_inc(s_slab[j], 16)
                with sp.Fori(0, 4) as i:
                    for j in range(4):
                        sp.wait_ge(s_used[j], i + (SGR["ffn"] + gd))
                        sp.dma_start(RING[:, j, 0:n * P].rearrange("p (t n) -> p t n", t=n),
                                     w_tiles(A["w_ffn_down"][0])[:, f0:f0 + n, ds(i * 512 + j * P, P)]).then_inc(s_slab[j], 16)

        @block.tensor
        def _(pe):
            def tr_bank(k):
                if k >= 2:
                    pe.wait_ge(s_te[k % 2], k // 2)

            def turn(dst, src):
                n = src.shape[0]
                return pe.transpose(dst, src, IDENT[0:n, 0:n])

            def tile(j, n, lhs, rhs):
                for kt in range(n):
                    for h in range(2):
                        mm = pe.matmul(PS[:, 2 * j + h, 0:HALF], lhs(kt), rhs(kt, h), start=(kt == 0), stop=(kt == n - 1))
                return mm

            def groups(n, sg, pg, kts, width, rhs):
                def group(i):
                    for j in range(4):
                        pe.wait_ge(s_slab[j], i * 16 + 16 * (sg + 1))
                        if type(i) is not int:
                            pe.wait_ge(s_ps[j], i + pg)
                        w = RING[:, j, 0:kts * P].rearrange("p (t n) -> p t n", t=kts)
                        tile(j, kts, lambda kt: w[:, kt, :], rhs).then_inc(s_used[j], 1)

                steps(pe, n, group, peel=pg == 0)

            def norm_sum(name, src=None):
                _, base, n = NRM[name]
                for kt in range(n):
                    if src is None:
                        pe.wait_ge(s_sq, base + kt + 1 - 8 * (name not in ("mix",)))
                        t = SQ[(base + kt) % 2]
                    else:
                        t = src(kt)
                    for h in range(2):
                        mm = pe.matmul(PS[:, h, 0:HALF], ONES[:, :], t[:, h * HALF:(h + 1) * HALF],
                                       start=(kt == 0), stop=(kt == n - 1))
                    mm.then_inc(s_ss, 1)

            def hrhs(src):
                return lambda kt, h: src[:, kt, h * HALF:(h + 1) * HALF]

            pe.wait_ge(s_const, 16)
            for tt in range(5):
                pe.wait_ge(s_x[tt], 16)
                n = P if tt < 4 else SAMP
                src = X4[tt] if tt < 4 else XS
                for m in range(4):
                    k = jobs["x"] + 4 * tt + m
                    tr_bank(k)
                    for a in range(4):
                        ins = turn(bank(k)[:, a * P:a * P + n], src[:, (4 * m + a) * P:(4 * m + a + 1) * P])
                    ins.then_inc(s_tr, 1)
            pe.wait_ge(s_rows, 16 * 18)
            k = jobs["vec"]
            tr_bank(k)
            for a in range(KT):
                ins = turn(bank(k)[:, 6 * a:6 * a + 6], VECR[:, a * P:(a + 1) * P])
            ins.then_inc(s_tr, 1)
            k = jobs["conv"]
            tr_bank(k)
            for a in range(CT):
                ins = turn(bank(k)[:, 35 * a:35 * a + 35], CONVR[:, a * P:(a + 1) * P])
            ins.then_inc(s_tr, 1)
            for m in range(4):
                k = jobs["state"] + m
                tr_bank(k)
                for a in range(2):
                    for hb in range(2):
                        ins = turn(bank(k)[:, a * 240 + hb * 120:a * 240 + hb * 120 + 120],
                                   STR_[:, hb, (2 * m + a) * P:(2 * m + a + 1) * P])
                ins.then_inc(s_tr, 1)
            k = jobs["cmpp"]
            tr_bank(k)
            turn(bank(k)[:, 0:68], CMPR).then_inc(s_tr, 1)

            pe.wait_ge(s_ones, 1)
            norm_sum("mix")
            pe.wait_ge(s_h, 16)
            turned(pe, end_of("cmpp"))
            pe.wait_ge(s_wg, 48)
            for kt in range(KT):
                for h in range(2):
                    mm = pe.matmul(PS[0:GATES, 2 + h, 0:HALF], WG[:, kt, :], HTL[:, kt, h * HALF:(h + 1) * HALF],
                                   start=(kt == 0), stop=(kt == KT - 1))
            mm.then_inc(s_gm, 1)
            pe.wait_ge(s_gs, 1)
            groups(4, SGR["glu"], PGR["glu"], KT, P, hrhs(HTL))
            groups(5, SGR["qkv"], PGR["qkv"], KT, P, hrhs(HTL))

            for j in range(4):
                pe.wait_ge(s_ps[j], PGR["out"])
            k = jobs["gate"]
            tr_bank(k)
            for tt in range(5):
                n = P if tt < 4 else SAMP
                ins = turn(bank(k)[0:n, tt * GATES:(tt + 1) * GATES], GT[:, tt * P:tt * P + n])
            ins.then_inc(s_tr, 1)
            for tt in range(5):
                n = P if tt < 4 else SAMP
                for m in range(3):
                    k = jobs["kvtok"] + 3 * tt + m
                    tr_bank(k)
                    for a in range(4):
                        ins = turn(bank(k)[0:n, a * P:(a + 1) * P], C[:, T_KC + 4 * m + a, tt * P:tt * P + n])
                    ins.then_inc(s_tr, 1)
            pe.wait_ge(s_u, CT)
            for which in range(2):
                for m in range(2):
                    k = jobs["ucap"] + 2 * which + m
                    tr_bank(k)
                    for a in range(4):
                        src = UC[:, 4 * m + a, 0:PREV] if which == 0 else UC[:, 4 * m + a, PREV:PREV + SAMP]
                        n = PREV if which == 0 else SAMP
                        ins = turn(bank(k)[0:n, a * P:(a + 1) * P], src)
                    ins.then_inc(s_tr, 1)
            turned(pe, end_of("gate"))
            for g in range(GQA):
                gsrc = GTOK[0:SAMP, 4, :].rearrange("p (k g j) -> p k g j", k=KV, g=GQA)[:, :, g, :]
                mm = pe.matmul(PS[:, 4, 0:6].rearrange("p (k j) -> p k j", k=KV), SELG[:, g, :], gsrc, start=(g == 0), stop=(g == GQA - 1))
            mm.then_inc(s_gm, 1)

            pe.wait_ge(s_cv, CT)
            norm_sum("lnmu", lambda kt: MIX[:, CT + kt, :])
            pe.wait_ge(s_mu, 1)
            norm_sum("lnvar")
            norm_sum("gconv")

            def w2_out(n):
                if n >= 1:
                    pe.wait_ge(s_cwr, n)

            def second_layer(p_):
                kind, half = divmod(p_, 2)
                first = {0: 0, 1: 2, 2: 3, 3: 6}[p_]
                pe.wait_ge(s_ge, (3, 5, 8, 10)[p_])
                if kind == 0:
                    w2_out(first)
                    for f in range(HT):
                        mm = pe.matmul(PS[:, 5, 0:SEG * NC_S], W2[:, 0, f, :], HIDS[:, f, :], start=(f == 0), stop=(f == 1))
                    mm.then_inc(s_cw, 1)
                else:
                    for q in range(2):
                        w2_out(first + q)
                        for s in range(4):
                            for f in range(HT):
                                sg_ = 4 * q + s
                                mm = pe.matmul(PS[0:NC_S, 5, s * DH:(s + 1) * DH], HIDS[:, f, sg_ * NC_S:(sg_ + 1) * NC_S],
                                               W2[:, 1, f, :], start=(f == 0), stop=(f == 1))
                        mm.then_inc(s_cw, 1)
                if half == 0:
                    w2_out(1 if kind == 0 else 5)
                    if kind == 0:
                        for f in range(HT):
                            mm = pe.matmul(PS[:, 5, 0:KV * NC_P], W2[:, 0, f, :], HIDP[:, f, :], start=(f == 0), stop=(f == 1))
                    else:
                        for kv in range(KV):
                            for f in range(HT):
                                mm = pe.matmul(PS[0:NC_P, 5, kv * DH:(kv + 1) * DH], HIDP[:, f, kv * NC_P:(kv + 1) * NC_P],
                                               W2[:, 1, f, :], start=(f == 0), stop=(f == 1))
                    mm.then_inc(s_cw, 1)

            pe.wait_ge(s_w2, 32)
            step = 0
            for p_ in range(4):
                kind, half = divmod(p_, 2)
                for b in range(4):
                    for pg4 in range(2):
                        pe.wait_ge(s_pg[step % 2], 64 * (step // 2 + 1))
                        for kv in range(KV):
                            k = jobs["pages"] + 2 * step + kv
                            tr_bank(k)
                            for a in range(4):
                                ins = turn(bank(k)[:, a * P:(a + 1) * P], PGS[step % 2][:, a, kv * DH:(kv + 1) * DH])
                            ins.then_inc(s_tr, 1)
                        step += 1
                if p_:
                    second_layer(p_ - 1)
                w1 = RING[:, :, :].rearrange("p a (l f) -> p (a l) f", l=8)
                if half == 0:
                    pe.wait_ge(s_kp, kind + 1)
                    for j in range(4):
                        pe.wait_ge(s_slab[j], 16 * (SGR["w1k"] + kind + 1))
                    if kind:
                        pe.wait_ge(s_cb, 1)
                    for f in range(HT):
                        for l in range(BLK):
                            n0 = l // STR
                            mm = pe.matmul(PS[:, 4, f * P:f * P + 93].rearrange("p (s n) -> p s n", s=3), w1[:, l, f * P:(f + 1) * P],
                                           KP[:, l % STR, :, n0:n0 + NC_P], start=(l == 0), stop=(l == BLK - 1))
                    mm.then_inc(s_cp, 1)
                turned(pe, jobs["pages"] + 16 * (p_ + 1))
                for l in range(BLK):
                    n0 = l // STR
                    for f in range(HT):
                        mm = pe.matmul(PS[:, 2 * half + f, 0:SEG * NC_S].rearrange("p (s n) -> p s n", s=SEG), w1[:, l, f * P:(f + 1) * P],
                                       KX[:, l % STR, :, n0:n0 + NC_S], start=(l == 0), stop=(l == BLK - 1))
                    if half == 1 and l % 8 == 7:
                        mm.then_inc(s_used[l // 8], 1)
                if half == 0:
                    mm.then_inc(s_cg, 1)
            second_layer(3)

            def scores(u):
                kv, qb = UNITS[u]
                n = (qb + 1) * P
                if u:
                    pe.wait_ge(s_ccr, u)
                at = 2 * SEG * NC_S + kv * NC_P
                for h in range(GQA):
                    mm = pe.matmul(PS[:, 4, h * 32:h * 32 + NC_P], C[:, kv * GQA + h, qb * P:(qb + 1) * P], KC[:, at:at + NC_P],
                                   start=True, stop=True)
                mm.then_inc(s_csc, 1)
                for h in range(GQA):
                    s = 4 * u + h
                    if s >= 2:
                        pe.wait_ge(s_scr, s - 1)
                    q = C[:, kv * GQA + h, qb * P:(qb + 1) * P]
                    pe.matmul(PS[:, 2 * (s % 2), 0:n], q, C[:, T_KW + kv, 0:n], start=True, stop=True)
                    pe.matmul(PS[:, 2 * (s % 2) + 1, 0:n], q, C[:, T_KS + kv, 0:n], start=True, stop=True).then_inc(s_sc, 1)

            def values(u):
                pieces = attn_pieces(u)
                pe.wait_ge(s_pn, 12 * (u + 1))
                if u:
                    pe.wait_ge(s_ov, u)

                def product(m):
                    k = UJOB[u] + m
                    pe.wait_ge(s_te[k % 2], k // 2 + 1)
                    return pe.matmul(PS[:, 5, :], pieces[m][2], PT_[m][0:pieces[m][1], :], start=(m == 0), stop=(m == len(pieces) - 1))

                for m, (col, n, _) in enumerate(pieces):
                    k = UJOB[u] + m
                    tr_bank(k)
                    for h in range(GQA):
                        ins = turn(bank(k)[0:n, h * P:(h + 1) * P], PBUF[u % 2][:, h, col:col + n])
                    ins.then_inc(s_tr, 1)
                    if m >= 2:
                        product(m - 2)
                product(len(pieces) - 2)
                product(len(pieces) - 1).then_inc(s_pv, 1)

            pe.wait_ge(s_cwr, 8)
            pe.wait_ge(s_ge, 10)
            pe.wait_ge(s_gs, 2)
            for u in range(8):
                scores(u)
                if u:
                    values(u - 1)
            values(7)

            pe.wait_ge(s_q, 1)
            pe.wait_ge(s_scr, 32)
            pe.wait_ge(s_ov, 8)
            for kv in range(KV):
                for b in range(NB):
                    at = (b * KV + kv) * NC_S
                    pe.matmul(PS[:, kv, 0:NC_S], QP[:, kv, b, :], KC[:, at:at + NC_S], start=(b == 0), stop=(b == NB - 1))
                pe.matmul(PS[:, kv, 64:96], QA[:, kv, :], C[:, T_KS + kv, SEQ:TOK], start=True, stop=True)
                pe.matmul(PS[:, kv, 96:128], QA[:, kv, :], C[:, T_KW + kv, SEQ:TOK], start=True, stop=True).then_inc(s_s1, 1)
            for kv in range(KV):
                pe.wait_ge(s_ss_, 1)
                for gated in range(2):
                    k = jobs["s_cmp"] + 2 * kv + gated
                    tr_bank(k)
                    turn(bank(k)[0:NC_S, 0:P], PSC[:, kv, gated, :]).then_inc(s_tr, 1)
            turned(pe, end_of("s_cmp"))
            for kv in range(KV):
                pe.matmul(PS[:, 2, kv * 32:kv * 32 + N_SEL], PCT[0:NC_S, kv, :], cst("overlap", NC_S), start=True, stop=True).then_inc(s_im, 1)
            pe.wait_ge(s_imr, 1)
            for kv in range(KV):
                pe.matmul(PS[:, 3, kv * 32:kv * 32 + N_SEL], cst("group"), IMP[:, kv, :], start=True, stop=True).then_inc(s_im, 1)
            kt_win = KTS[0].rearrange("p (s k t) -> p s k t", s=2, k=2)
            for b in range(NB + 1):
                if b < NB:
                    pe.wait_ge(s_sraw[b % 2], 16 * (b // 2 + 1))
                    for kv in range(KV):
                        k = jobs["s_win"] + 2 * b + kv
                        tr_bank(k)
                        for a in range(4):
                            ins = turn(bank(k)[:, a * P:(a + 1) * P], WRAW[b % 2][:, a, kv * DH:(kv + 1) * DH])
                        ins.then_inc(s_tr, 1)
                if b:
                    turned(pe, jobs["s_win"] + 2 * b)
                    for kv in range(KV):
                        mm = pe.matmul(PS[:, 4 + kv, :], QP[:, kv, b - 1, :], kt_win[:, (b - 1) % 2, kv, :], start=(b == 1), stop=(b == NB))
                    mm.then_inc(s_kt, 1)
            pe.wait_ge(s_imr, 2)
            kt_sel = KTS[0].rearrange("p (k h t) -> p k h t", k=2, h=2)
            for b in range(NB):
                pe.wait_ge(s_sraw[b % 2], 16 * 4 + 128 * (b // 2 + 1))
                for kv in range(KV):
                    for h in range(2):
                        k = jobs["s_sel"] + 4 * b + 2 * kv + h
                        tr_bank(k)
                        for a in range(4):
                            at = (4 * h + a) * KVW + kv * DH
                            ins = turn(bank(k)[:, a * P:(a + 1) * P], SRAW[b % 2][:, at:at + DH])
                        ins.then_inc(s_tr, 1)
                turned(pe, jobs["s_sel"] + 4 * (b + 1))
                for kv in range(KV):
                    for h in range(2):
                        mm = pe.matmul(PS[:, 2 * kv + h, :], QP[:, kv, b, :], kt_sel[:, kv, h, :], start=(b == 0), stop=(b == NB - 1))
                mm.then_inc(s_kt, 1)
            pe.wait_ge(s_ss_, 2)
            for kv in range(KV):
                for m in range(4):
                    k = jobs["s_p"] + 4 * kv + m
                    tr_bank(k)
                    if m < 2:
                        cols = [PSS[:, kv, (4 * m + a) * P:(4 * m + a + 1) * P] for a in range(4)]
                    elif m == 2:
                        cols = [PSW[:, kv, a * P:(a + 1) * P] for a in range(4)]
                    else:
                        cols = [PSS[:, kv, PAST:PAST + SAMP], PSW[:, kv, WIN:WIN + SAMP]]
                    for a, src in enumerate(cols):
                        n = src.shape[1]
                        ins = turn(bank(k)[0:n, a * P:(a + 1) * P], src)
                    ins.then_inc(s_tr, 1)
            turned(pe, end_of("s_p"))
            for b in range(NB):
                pe.wait_ge(s_sraw[0], 16 * 4 + 128 * (4 + b + 1))
                pe.wait_ge(s_sraw[1], 16 * 4 + 128 * 4 + 16 * (b + 1))
                if b >= 2:
                    pe.wait_ge(s_sor, b - 1)
                for kv in range(KV):
                    out = PS[:, 2 * (b % 2) + kv, 0:P]
                    terms = [(VC[0:NC_S, b * KV + kv, :], PTS[0:NC_S, kv, 14, :]),
                             (VT[0:SAMP, 4, kv, :], PTS[0:SAMP, kv, 8, :]), (VT[0:SAMP, 4, 2 + kv, :], PTS[0:SAMP, kv, 13, :])]
                    terms += [(SRAW[0][:, a * KVW + kv * DH:a * KVW + (kv + 1) * DH], PTS[:, kv, a, :]) for a in range(8)]
                    terms += [(WRAW[1][:, a, kv * DH:(kv + 1) * DH], PTS[:, kv, 9 + a, :]) for a in range(4)]
                    for m, (v, p) in enumerate(terms):
                        mm = pe.matmul(out, v, p, start=(m == 0), stop=(m == len(terms) - 1))
                mm.then_inc(s_so, 1)

            pe.wait_ge(s_sor, NB)
            norm_sum("gattn")
            pe.wait_ge(s_h, HBASE["mem"])
            groups(4, SGR["out"], PGR["out"], KT, P, hrhs(MIX))

            pe.wait_ge(s_mn, 2)
            for tt in range(2):
                for m in range(4):
                    k = jobs["memr"] + 4 * tt + m
                    tr_bank(k)
                    if k - jobs["memr"] < 2:
                        pe.wait_ge(s_ps[3], PGR["mq"])
                    for a in range(4):
                        ins = turn(bank(k)[:, a * P:(a + 1) * P], MR[tt][:, (4 * m + a) * P:(4 * m + a + 1) * P])
                    ins.then_inc(s_tr, 1)
            turned(pe, end_of("memr"))
            for j in range(2):
                pe.wait_ge(s_ps[j], PGR["mq"])
            for kind in range(2):
                for j in range(4):
                    pe.wait_ge(s_slab[j], 16 * (SGR["mk"] + kind + 1))
                    w = RING[:, j, :].rearrange("p (t n) -> p t n", t=4)
                    for a in range(4):
                        for tt in range(2):
                            kt = 4 * j + a
                            mm = pe.matmul(PS[:, 2 * kind + tt, :], MT[:, kt, tt * P:(tt + 1) * P], w[:, a, :],
                                           start=(kt == 0), stop=(kt == KT - 1))
                    mm.then_inc(s_used[j], 1)
            for tt in range(2):
                k = jobs["memk"] + tt
                tr_bank(k)
                pe.wait_ge(s_mke, 1)
                for a in range(4):
                    ins = turn(bank(k)[:, a * P:(a + 1) * P], KMT[:, tt, a * P:(a + 1) * P])
                ins.then_inc(s_tr, 1)

            norm_sum("mem")
            pe.wait_ge(s_h, HBASE["ffn"])
            turned(pe, end_of("memk"))
            pe.wait_ge(s_mke, 2)
            groups(1, SGR["mq"], PGR["mq"], KT, P, hrhs(HTL))
            for j in range(4):
                pe.wait_ge(s_ps[j], PGR["mo"])

            def mem_scores(u):
                if u >= 2:
                    pe.wait_ge(s_mex, u - 1)
                for h in range(MH):
                    mm = pe.matmul(PS[:, 2 * (u % 2) + h // 2, (h % 2) * NMEM:(h % 2 + 1) * NMEM], QM[:, h, u * P:(u + 1) * P],
                                   KMD[:, h, :], start=True, stop=True)
                mm.then_inc(s_msc, 1)

            def mem_values(u):
                pe.wait_ge(s_mpn, u + 1)
                if u >= 2:
                    pe.wait_ge(s_mov, u - 1)
                for m in range(2):
                    k = jobs["mp"] + 2 * u + m
                    tr_bank(k)
                    for a in range(2):
                        for st in range(2):
                            ins = turn(bank(k)[:, (2 * a + st) * P:(2 * a + st + 1) * P], PMB[u % 2][:, 2 * m + a, st * P:(st + 1) * P])
                    ins.then_inc(s_tr, 1)
                for m in range(2):
                    k = jobs["mp"] + 2 * u + m
                    pe.wait_ge(s_te[k % 2], k // 2 + 1)
                    for a in range(2):
                        h = 2 * m + a
                        for st in range(2):
                            mm = pe.matmul(PS[:, 4 + u % 2, h * P:(h + 1) * P], VMT[:, st, h * DH:(h + 1) * DH], PMT[m][:, a, st, :],
                                           start=(st == 0), stop=(st == 1))
                mm.then_inc(s_mpv, 1)

            for u in range(QB):
                mem_scores(u)
                if u:
                    mem_values(u - 1)
            mem_values(QB - 1)
            pe.wait_ge(s_qmp, 1)
            pe.wait_ge(s_mex, QB)
            for b in range(NB + 1):
                if b < NB:
                    pe.wait_ge(s_kmr[b % 2], 16 * (b // 2 + 1))
                    for tt in range(2):
                        k = jobs["ms"] + 2 * b + tt
                        tr_bank(k)
                        for a in range(4):
                            ins = turn(bank(k)[:, a * P:(a + 1) * P], KMR[b % 2][:, tt, a * P:(a + 1) * P])
                        ins.then_inc(s_tr, 1)
                if b:
                    turned(pe, jobs["ms"] + 2 * b)
                    for h in range(MH):
                        mm = pe.matmul(PS[h * SAMP:(h + 1) * SAMP, 0, 0:NMEM], QMP[:, h, b - 1, :], KMS[(b - 1) % 2][:, h, :],
                                       start=(b == 1), stop=(b == NB))
                    mm.then_inc(s_msc, 1)
            pe.wait_ge(s_mpn, QB + 1)
            k = jobs["msp"]
            tr_bank(k)
            for st in range(2):
                ins = turn(bank(k)[:, st * P:(st + 1) * P], PMS[:, st * P:(st + 1) * P])
            ins.then_inc(s_tr, 1)
            turned(pe, end_of("msp"))
            for b in range(NB):
                pe.wait_ge(s_vmr[b % 2], 16 * (b // 2 + 1))
                for h in range(MH):
                    at = h * SAMP + b * NT
                    for st in range(2):
                        mm = pe.matmul(PS[:, 2, at:at + NT], VMR[b % 2][:, st, h * DH:(h + 1) * DH], PMST[:, st, at:at + NT],
                                       start=(st == 0), stop=(st == 1))
                mm.then_inc(s_mpv, 1)
            pe.wait_ge(s_mov, QB + 1)
            for m in range(4):
                pe.wait_ge(s_slab[m], 16 * (SGR["mo"] + 1))
                w = RING[:, m, :].rearrange("p (t n) -> p t n", t=4)
                for j in range(4):
                    pe.wait_ge(s_ps[j], PGR["mo"] + m)
                    tile(j, MH, lambda kt: w[:, kt, j * P:(j + 1) * P], hrhs(QM)).then_inc(s_used[m] if j == 3 else s_mop, 1)

            pe.wait_ge(s_ps[0], PGR["ffn"])
            norm_sum("ffn")
            pe.wait_ge(s_fr, 48)
            pe.wait_ge(s_ps[3], PGR["ffn"])
            for m in range(2):
                k = jobs["ffp"] + m
                tr_bank(k)
                for a in range(22):
                    ins = turn(bank(k)[:, 20 * a:20 * a + 20], FR[:, (22 * m + a) * P:(22 * m + a + 1) * P])
                ins.then_inc(s_tr, 1)
            pe.wait_ge(s_h, HBASE["final"])
            turned(pe, end_of("ffp"))
            for f0, n, gu, gd in ffn_plan:
                groups(n // 2, SGR["ffn"] + gu, PGR["ffn"] + gu, KT, P, hrhs(HTL))
                for t in range(2):
                    pe.wait_ge(s_ps[2 * t + 1], PGR["ffn"] + gd)
                groups(4, SGR["ffn"] + gd, PGR["ffn"] + gd, n, P, hrhs(AT))
            for j in range(4):
                pe.wait_ge(s_ps[j], PGR["ffn"] + 38)
            for m in range(11):
                k = jobs["ffs"] + m
                tr_bank(k)
                for a in range(4):
                    ins = turn(bank(k)[0:18, a * P:(a + 1) * P], GSV[:, 4 * m + a, :])
                ins.then_inc(s_tr, 1)
            norm_sum("final")
            pe.wait_ge(s_h, HBASE["final"] + KT)
            for tt in range(5):
                n = P if tt < 4 else SAMP
                for m in range(4):
                    k = jobs["y"] + 4 * tt + m
                    tr_bank(k)
                    for a in range(4):
                        ins = turn(bank(k)[0:n, a * P:(a + 1) * P], HTL[:, 4 * m + a, tt * P:tt * P + n])
                    ins.then_inc(s_tr, 1)


        @block.scalar
        def _(act):
            def turned_tile(k, job):
                if k % 2 == 0:
                    act.wait_ge(s_tr, k + 1)
                    for dst, src in job(k):
                        ins = act.activation(dst, src, ACT.Copy)
                    ins.then_inc(s_te[0], 1)

            def turned_tiles(name, job):
                for k in range(jobs[name], end_of(name)):
                    turned_tile(k, job)

            def squares(name, src, ready):
                _, base, n = NRM[name]
                for kt in range(n):
                    ready(kt)
                    if base + kt >= 2:
                        act.wait_ge(s_ss, base + kt - 1)
                    act.activation(SQ[(base + kt) % 2], src(kt), ACT.Square).then_inc(s_sq, 1)
                act.wait_ge(s_ss, base + n)
                if ROOTS[name]:
                    act.wait_ge(s_rs, ROOTS[name])
                act.activation(halves(SG[:, :]), PAIR[0], ACT.Sqrt, bias=cst("eps"), scale=1.0 / (n * P)).then_inc(s_rt, 1)

            turned_tiles("x", x_job)
            turned_tiles("vec", vec_job)
            turned_tiles("conv", conv_job)
            turned_tiles("state", state_job)
            turned_tiles("cmpp", cmpp_job)
            act.wait_ge(s_const, 16)
            turned(act, end_of("x"))
            squares("mix", lambda kt: XT[:, kt, :], lambda kt: None)
            act.wait_ge(s_gm, 1)
            act.wait_ge(s_wg, 48)
            act.activation(halves(GT), PS[0:GATES, 2:4, 0:HALF], ACT.Sigmoid, bias=BG[:, :]).then_inc(s_gs, 1)
            act.wait_ge(s_rs, 1)
            def glu_gate(i):
                for t in range(2):
                    act.wait_ge(s_used[2 * t + 1], i + 1)
                    if t or type(i) is not int:
                        act.wait_ge(s_u, i * 2 + t)
                    act.activation(halves(SG[:, :]), PAIR[2 * t + 1], ACT.Sigmoid).then_inc(s_sg, 1)

            steps(act, 4, glu_gate, peel=True)
            with act.Fori(0, 5) as i:
                for j in range(4):
                    act.wait_ge(s_used[j], i + (SGR["qkv"] + 1))
                    act.activation(C[:, ds(i * 4 + j, 1), :].rearrange("p o (h t) -> p (o h) t", h=2), PAIR[j], ACT.Copy).then_inc(s_ps[j], 1)
            turned_tiles("gate", gate_job)
            turned_tiles("kvtok", kvtok_job)
            turned_tiles("ucap", ucap_job)
            act.wait_ge(s_gm, 2)
            act.activation(GSMP[:, :, :].rearrange("p k j -> p (k j)"), PS[:, 4, 0:6], ACT.Copy).then_inc(s_gs, 1)
            squares("lnvar", lambda kt: MIX[:, CT + kt, :], lambda kt: act.wait_ge(s_mu, kt + 1))
            for kt in range(CT):
                act.wait_ge(s_yl, kt + 1)
                act.activation(MIX[:, CT + kt, :], MIX[:, CT + kt, :], ACT.Silu, bias=CONVP[:, kt, 33:34]).then_inc(s_y, 1)
            squares("gconv", lambda kt: MIX[:, CT + kt, :], lambda kt: act.wait_ge(s_y, kt + 1))

            act.wait_ge(s_tok, 16 * N_TOK)
            act.wait_ge(s_rs, 3)
            reads = [0]

            def w2_read(dst, src):
                act.wait_ge(s_cw, reads[0] + 1)
                act.activation(dst, src, ACT.Copy).then_inc(s_cwr, 1)
                reads[0] += 1

            def second_out(p_):
                kind, half = divmod(p_, 2)
                if kind == 0:
                    w2_read(KC[:, half * SEG * NC_S:(half + 1) * SEG * NC_S], PS[:, 5, 0:SEG * NC_S])
                    if half == 0:
                        w2_read(KC[:, 2 * SEG * NC_S:2 * SEG * NC_S + KV * NC_P], PS[:, 5, 0:KV * NC_P])
                    return
                for q in range(2):
                    w2_read(VC[0:NC_S, half * SEG + 4 * q:half * SEG + 4 * q + 4, :],
                            PS[0:NC_S, 5, :].rearrange("p (s d) -> p s d", s=4))
                if half == 0:
                    w2_read(VCP[0:NC_P], PS[0:NC_P, 5, 0:KV * DH].rearrange("p (s d) -> p s d", s=KV))

            for p_ in range(4):
                kind, half = divmod(p_, 2)
                for k in range(jobs["pages"] + 16 * p_, jobs["pages"] + 16 * (p_ + 1)):
                    turned_tile(k, pages_job)
                if p_:
                    second_out(p_ - 1)
                if half == 0:
                    act.wait_ge(s_cb, kind + 1)
                    for f in range(HT):
                        ins = act.activation(HIDP[:, f, :], PS[:, 4, f * P:f * P + KV * NC_P], ACT.Gelu_apprx_tanh, bias=BIAS[:, f:f + 1])
                    ins.then_inc(s_ge, 1)
                    act.wait_ge(s_cg, kind + 1)
                else:
                    act.wait_ge(s_used[3], SGR["w1k"] + kind + 1)
                for f in range(HT):
                    act.activation(HIDS[:, f, :], PS[:, 2 * half + f, 0:SEG * NC_S], ACT.Gelu_apprx_tanh, bias=BIAS[:, f:f + 1]).then_inc(s_ge, 1)
            second_out(3)

            for u in range(9):
                if u < 8:
                    n = (UNITS[u][1] + 1) * P
                    act.wait_ge(s_nm, u + 1)
                    for h in range(GQA):
                        for br, (a, m) in enumerate(((0, n), (512, n), (1024, NC_P))):
                            v, c = PBUF[u % 2][:, h, a:a + m], 3 * h + br
                            act.activation(v, v, ACT.Exp, bias=NM[:, u % 2, c:c + 1], scale=SCALE,
                                           accum_out=SUM[:, u % 2, c:c + 1]).then_inc(s_ex, 1)
                if u:
                    if u >= 2:
                        act.wait_ge(s_pv, u - 1)
                    for k in range(UJOB[u - 1], UJOB[u - 1] + len(attn_pieces(u - 1))):
                        turned_tile(k, attn_job)
                    kv, qb = UNITS[u - 1]
                    act.wait_ge(s_pv, u)
                    act.activation(C[:, kv * GQA:(kv + 1) * GQA, qb * P:(qb + 1) * P],
                                   PS[:, 5, :].rearrange("p (g q) -> p g q", g=GQA), ACT.Copy).then_inc(s_ov, 1)

            act.wait_ge(s_smx, 1)
            for kv in range(KV):
                act.activation(PSC[:, kv, 0, :], PSC[:, kv, 0, :], ACT.Exp, bias=SNM[:, kv:kv + 1], scale=SCALE,
                               accum_out=SSM[:, kv:kv + 1]).then_inc(s_se, 1)
            turned_tiles("s_cmp", s_job)
            for b in range(NB):
                if b >= 2:
                    act.wait_ge(s_kt, b - 1)
                for k in range(jobs["s_win"] + 2 * b, jobs["s_win"] + 2 * b + 2):
                    turned_tile(k, s_job)
            for b in range(NB):
                act.wait_ge(s_kt, NB + b)
                for k in range(jobs["s_sel"] + 4 * b, jobs["s_sel"] + 4 * b + 4):
                    turned_tile(k, s_job)
            act.wait_ge(s_smx, 2)
            for kv in range(KV):
                act.activation(PSS[:, kv, :], PSS[:, kv, :], ACT.Exp, bias=SNM[:, 2 + kv:3 + kv], scale=SCALE,
                               accum_out=SSM[:, 2 + kv:3 + kv]).then_inc(s_se, 1)
                act.activation(PSW[:, kv, :], PSW[:, kv, :], ACT.Exp, bias=SNM[:, 4 + kv:5 + kv], scale=SCALE,
                               accum_out=SSM[:, 4 + kv:5 + kv]).then_inc(s_se, 1)
            turned_tiles("s_p", s_job)

            act.wait_ge(s_sor, NB)
            squares("gattn", lambda kt: C[:, kt, :], lambda kt: None)
            act.wait_ge(s_mr, 32)
            for tt in range(2):
                if tt:
                    act.wait_ge(s_msum, tt)
                act.activation(MSCR, MR[tt], ACT.Square, accum_out=MSQ[:, tt:tt + 1]).then_inc(s_msum, 1)
            act.wait_ge(s_msum, 2)
            act.activation(MRT, MSQ, ACT.Sqrt, bias=cst("eps"), scale=1.0 / D).then_inc(s_mrt, 1)
            act.wait_ge(s_h, HBASE["mem"])
            for k in range(jobs["memr"], end_of("memr")):
                if k % 2 == 0:
                    act.wait_ge(s_tr, k + 1)
                    dst, src = mem_job(k)[0]
                    m = (k - jobs["memr"]) % 4
                    for a in range(4):
                        ins = act.activation(dst[:, a, :], src[:, a, :], ACT.Copy, scale=VEC[:, 4 * m + a, 2:3])
                    ins.then_inc(s_te[0], 1)
            for kind, dst in ((0, KMT), (1, VMT)):
                act.wait_ge(s_used[3], SGR["mk"] + kind + 1)
                act.activation(dst, PS[:, 2 * kind:2 * kind + 2, :], ACT.Copy).then_inc(s_mke, 1)
            turned_tiles("memk", mem_job)

            squares("mem", lambda kt: XT[:, kt, :], lambda kt: act.wait_ge(s_ps[kt % 4], PGR["out"] + kt // 4 + 1))
            for j in range(4):
                act.wait_ge(s_used[j], SGR["mq"] + 1)
                act.activation(halves(QM[:, j, :]), PAIR[j], ACT.Copy).then_inc(s_ps[j], 1)
            for u in range(QB + 1):
                if u < QB:
                    act.wait_ge(s_mnm, u + 1)
                    if u >= 2:
                        act.wait_ge(s_tr, jobs["mp"] + 2 * (u - 1))
                    for h in range(MH):
                        ins = act.activation(PMB[u % 2][:, h, :], PS[:, 2 * (u % 2) + h // 2, (h % 2) * NMEM:(h % 2 + 1) * NMEM],
                                             ACT.Exp, bias=MNM[:, u % 2, h:h + 1], scale=SCALE, accum_out=MSU[:, u % 2, h:h + 1])
                    ins.then_inc(s_mex, 1)
                if u:
                    if u >= 2:
                        act.wait_ge(s_mpv, u - 1)
                    for k in range(jobs["mp"] + 2 * (u - 1), jobs["mp"] + 2 * u):
                        turned_tile(k, mem_job)
                    act.wait_ge(s_mpv, u)
                    act.activation(QM[:, :, (u - 1) * P:u * P], PS[:, 4 + (u - 1) % 2, :].rearrange("p (h q) -> p h q", h=MH),
                                   ACT.Copy).then_inc(s_mov, 1)
            for b in range(NB):
                if b >= 2:
                    act.wait_ge(s_msc, QB + b - 1)
                for k in (jobs["ms"] + 2 * b, jobs["ms"] + 2 * b + 1):
                    turned_tile(k, mem_job)
            act.wait_ge(s_mnm, QB + 1)
            act.activation(PMS, PS[:, 0, 0:NMEM], ACT.Exp, bias=MNM[:, 0, 0:1], scale=SCALE, accum_out=MSU[:, 0, 0:1]).then_inc(s_mex, 1)
            turned_tiles("msp", mem_job)
            act.wait_ge(s_mpv, QB + NB)
            act.activation(QM[:, :, SEQ:TOK], PS[:, 2, 0:P].rearrange("p (h r) -> p h r", h=MH), ACT.Copy).then_inc(s_mov, 1)

            squares("ffn", lambda kt: XT[:, kt, :], lambda kt: act.wait_ge(s_ps[kt % 4], PGR["mo"] + kt // 4 + 1))
            turned_tiles("ffp", ffp_job)
            for f0, n, gu, gd in ffn_plan:
                def gate_tiles(i, f0=f0, gu=gu):
                    for t in range(2):
                        f = i * 2 + (f0 + t)
                        act.wait_ge(s_used[2 * t], i + (SGR["ffn"] + gu + 1))
                        if type(i) is not int or f0:
                            act.wait_ge(s_fc, i * 2 + (f0 + t - 1))
                        first, second = PAIR[2 * t][:, 0, :], PAIR[2 * t][:, 1, :]
                        smp = second[:, SEQ - HALF:HALF].rearrange("p (b t) -> p b t", b=NB)
                        act.activation(GX[t][:, 2:2 + HALF], first, ACT.Copy)
                        act.activation(GX[t][:, 2 + HALF:2 + SEQ], second[:, 0:SEQ - HALF], ACT.Copy)
                        act.activation(GX[t][:, 2 + SEQ:].rearrange("p (b t) -> p b t", b=NB)[:, :, 2:6], smp, ACT.Copy).then_inc(s_gx, 1)
                        act.activation(GSV[:, ds(f, 1), 0:2].rearrange("p o t -> p (o t)"), second[:, SEQ - HALF - 2:SEQ - HALF], ACT.Copy)
                        act.activation(GSV[:, ds(f, 1), 2:18].rearrange("p o (b t) -> p (o b) t", b=NB), smp[:, :, 2:4],
                                       ACT.Copy).then_inc(s_ps[2 * t], 1)
                        act.wait_ge(s_fc, f + 1)
                        act.activation(FC[t], FC[t], ACT.Silu).then_inc(s_fs, 1)

                steps(act, n // 2, gate_tiles, peel=f0 == 0)
            turned_tiles("ffs", ffs_job)
            for j in range(4):
                act.wait_ge(s_ps[j], PGR["ffn"] + 38)
            squares("final", lambda kt: XT[:, kt, :], lambda kt: None)
            turned_tiles("y", y_job)

        @block.vector
        def _(dve):
            own = Chain(dve, s_dv)

            def turned_tile(k, job):
                if k % 2 == 1:
                    dve.wait_ge(s_tr, k + 1)
                    for dst, src in job(k):
                        ins = dve.tensor_copy(dst, src)
                    ins.then_inc(s_te[1], 1)

            def turned_tiles(name, job):
                for k in range(jobs[name], end_of(name)):
                    turned_tile(k, job)

            roots = [0]

            def inverse_root():
                roots[0] += 1
                dve.wait_ge(s_rt, roots[0])
                dve.reciprocal(RS[:, :], SG[:, :]).then_inc(s_rs, 1)
                dve.wait_ge(s_rs, roots[0])

            def normed(n, dst, src, gain):
                for kt in range(n):
                    dve.scalar_tensor_tensor(out=dst(kt), in0=src(kt), scalar=gain(kt), in1=RS[:, :], op0=ALU.mult, op1=ALU.mult).then_inc(s_h, 1)

            EXW = 2 * (PREV + SEQ + NB * (PREV + NT))
            ext_p = [EX[:, t, 0:PREV + SEQ] for t in range(2)]
            ext_s = [EX[:, t, PREV + SEQ:].rearrange("p (b t) -> p b t", b=NB) for t in range(2)]

            turned_tiles("x", x_job)
            turned_tiles("vec", vec_job)
            turned_tiles("conv", conv_job)
            turned_tiles("state", state_job)
            turned_tiles("cmpp", cmpp_job)
            turned(dve, end_of("cmpp"))
            inverse_root()
            normed(KT, lambda kt: HTL[:, kt, :], lambda kt: XT[:, kt, :], lambda kt: VEC[:, kt, 0:1])

            for t in range(2):
                own.step(dve.memset(ext_p[t][:, 0:PREV], 0.0))
            dve.wait_ge(s_h, KT)
            STEPS = 2 * (2 + 3 + 2 + (CW - 1) + 1 + 1)
            with dve.Fori(0, 4) as i:
                loop = Chain(dve, s_cvl, i * STEPS)
                for t in range(2):
                    ct = i * 2 + t
                    taps, E, S = CWT[:, t, :], ext_p[t], ext_s[t]
                    loop.tick(dve.tensor_copy(CWT[:, ds(t, 1), :], CONVP[:, ds(ct, 1), :]))
                    loop.tick(dve.tensor_copy(S[:, :, 0:PREV], STT[:, ds(ct, 1), :].rearrange("p o (b t) -> p (o b) t", b=NB)))
                    dve.wait_ge(s_used[2 * t], i + 1)
                    dve.wait_ge(s_sg, ct + 1)
                    first, second = PAIR[2 * t][:, 0, :], PAIR[2 * t][:, 1, :]
                    loop.tick(dve.tensor_tensor(E[:, PREV:PREV + HALF], first, SG[:, 0:HALF], ALU.mult))
                    loop.tick(dve.tensor_tensor(E[:, PREV + HALF:PREV + SEQ], second[:, 0:SEQ - HALF], SG[:, HALF:SEQ], ALU.mult))
                    loop.step(dve.tensor_tensor(S[:, :, PREV:PREV + NT], second[:, SEQ - HALF:HALF].rearrange("p (b t) -> p b t", b=NB),
                                                SG[:, SEQ:TOK].rearrange("p (b t) -> p b t", b=NB), ALU.mult))
                    dve.tensor_copy(UC[:, ds(ct, 1), 0:PREV].rearrange("p o t -> p (o t)"), E[:, SEQ:SEQ + PREV]).then_inc(s_ps[2 * t], 1)
                    dve.tensor_copy(UC[:, ds(ct, 1), PREV:].rearrange("p o (b t) -> p (o b) t", b=NB), S[:, :, PREV:]).then_inc(s_ps[2 * t + 1], 1)
                    off = t * (PREV + SEQ + NB * (PREV + NT)) + PREV + SEQ
                    win = bass.AP(EX, off, [[EXW, P], [PREV + NT, NB], [1, NT], [1, CW]])
                    tb = bass.AP(CWT, 35 * t, [[70, P], [0, NB], [0, NT], [1, CW]])
                    dve.tensor_tensor(PROD, win, tb, ALU.mult).then_inc(s_u, 1)
                    loop.tick(dve.tensor_scalar(RS[:, 0:SEQ], E[:, 0:SEQ], taps[:, 0:1], taps[:, CW:CW + 1], ALU.mult, ALU.add))
                    dve.wait_ge(s_u, ct + 1)
                    loop.tick(dve.tensor_reduce(RS[:, SEQ:TOK].rearrange("p (b t) -> p b t", b=NB), PROD, AX_X, ALU.add))
                    for w in range(1, CW):
                        loop.wait()
                        loop.tick(dve.scalar_tensor_tensor(out=RS[:, 0:SEQ], in0=E[:, w:w + SEQ], scalar=taps[:, w:w + 1],
                                                           in1=RS[:, 0:SEQ], op0=ALU.mult, op1=ALU.add))
                    loop.step(dve.tensor_scalar(RS[:, SEQ:TOK], RS[:, SEQ:TOK], taps[:, CW:CW + 1], None, ALU.add))
                    loop.tick(dve.tensor_copy(MIX[:, ds(ct + CT, 1), 0:HALF].rearrange("p o t -> p (o t)"), RS[:, 0:HALF]))
                    dve.tensor_copy(MIX[:, ds(ct + CT, 1), HALF:].rearrange("p o t -> p (o t)"), RS[:, HALF:TOK]).then_inc(s_cv, 1)

            turned_tiles("gate", gate_job)
            turned_tiles("kvtok", kvtok_job)
            turned_tiles("ucap", ucap_job)
            dve.wait_ge(s_ss, NRM["lnmu"][1] + CT)
            own.step(dve.tensor_scalar(halves(RS[:, :]), PAIR[0], 1.0 / CCH, None, ALU.mult))
            for kt in range(CT):
                dve.tensor_tensor(MIX[:, CT + kt, :], MIX[:, CT + kt, :], RS[:, :], ALU.subtract).then_inc(s_mu, 1)
            dve.wait_ge(s_mu, CT)
            inverse_root()
            for kt in range(CT):
                dve.scalar_tensor_tensor(out=MIX[:, CT + kt, :], in0=MIX[:, CT + kt, :], scalar=CONVP[:, kt, 32:33], in1=RS[:, :],
                                         op0=ALU.mult, op1=ALU.mult).then_inc(s_yl, 1)
            dve.wait_ge(s_yl, CT)
            inverse_root()
            normed(CT, lambda kt: MIX[:, CT + kt, :], lambda kt: MIX[:, CT + kt, :], lambda kt: CONVP[:, kt, 34:35])

            dve.wait_ge(s_tok, 16 * N_TOK)
            for p_ in range(4):
                kind, half = divmod(p_, 2)
                if half == 0:
                    if kind:
                        dve.wait_ge(s_cp, 1)
                    own.step(dve.memset(KP[:, :, 2, :], 0.0))
                    for kv in range(KV):
                        own.tick(dve.tensor_copy(KP[:, :, kv, :], C[:, T_KC + 2 * kind + kv, 0:SEQ].rearrange("p (c l) -> p l c", l=STR)))
                    own.step(dve.tensor_copy(KP[:, :, 2, 0], CMPP[:, 34 * kind:34 * kind + STR]))
                    dve.tensor_copy(KP[:, :, 2, 1], CMPP[:, 34 * kind + STR:34 * kind + BLK]).then_inc(s_kp, 1)
                for k in range(jobs["pages"] + 16 * p_, jobs["pages"] + 16 * (p_ + 1)):
                    turned_tile(k, pages_job)
                if half == 0:
                    dve.wait_ge(s_cp, kind + 1)
                    if kind:
                        dve.wait_ge(s_ge, 5)
                    at = 34 * kind + BLK
                    col = PS[:, 4, 0:2 * P].rearrange("p (f n) -> p f n", f=HT)[:, :, KV * NC_P]
                    dve.tensor_tensor(BIAS[:, :], col, CMPP[:, at:at + HT], ALU.add).then_inc(s_cb, 1)

            for u in range(9):
                if u < 8:
                    kv, qb = UNITS[u]
                    n = (qb + 1) * P
                    if u >= 2:
                        dve.wait_ge(s_tr, UJOB[u - 1])
                    dve.wait_ge(s_csc, u + 1)
                    for h in range(GQA):
                        ins = dve.tensor_tensor_reduce(PBUF[u % 2][:, h, 1024:1024 + NC_P], PS[:, 4, h * 32:h * 32 + NC_P],
                                                       cst("cmask")[:, qb * NC_P:(qb + 1) * NC_P], 1.0, NEG, ALU.add, ALU.max,
                                                       MX[:, u % 2, 3 * h + 2:3 * h + 3])
                        if h < GQA - 1:
                            own.tick(ins)
                    ins.then_inc(s_ccr, 1)
                    for h in range(GQA):
                        s = 4 * u + h
                        dve.wait_ge(s_sc, s + 1)
                        mask = cst("mask")[:, 640 - n:640]
                        for br, (a, src) in enumerate(((0, PS[:, 2 * (s % 2), 0:n]), (512, PS[:, 2 * (s % 2) + 1, 0:n]))):
                            ins = dve.tensor_tensor_reduce(PBUF[u % 2][:, h, a:a + n], src, mask, 1.0, NEG, ALU.add, ALU.max,
                                                           MX[:, u % 2, 3 * h + br:3 * h + br + 1])
                            if br == 0:
                                own.tick(ins)
                        ins.then_inc(s_scr, 1)
                    own.wait()
                    dve.wait_ge(s_ccr, u + 1)
                    dve.wait_ge(s_scr, 4 * (u + 1))
                    dve.tensor_scalar(NM[:, u % 2, :], MX[:, u % 2, :], FLOOR, -SCALE, ALU.max, ALU.mult).then_inc(s_nm, 1)
                if u:
                    if u >= 2:
                        dve.wait_ge(s_pv, u - 1)
                    for k in range(UJOB[u - 1], UJOB[u - 1] + len(attn_pieces(u - 1))):
                        turned_tile(k, attn_job)
                if u < 8:
                    dve.wait_ge(s_ex, 12 * (u + 1))
                    own.step(dve.tensor_scalar(FAC[:, u % 2, :], SUM[:, u % 2, :], 1e-30, None, ALU.max))
                    own.step(dve.reciprocal(FAC[:, u % 2, :], FAC[:, u % 2, :]))
                    fac = FAC[:, u % 2, :].rearrange("p (g j) -> p g j", j=3)
                    gates = GTOK[:, qb, :].rearrange("p (k g j) -> p k g j", k=KV, g=GQA)[:, kv]
                    for br in range(3):
                        own.tick(dve.tensor_tensor(fac[:, :, br], fac[:, :, br], gates[:, :, 2 - br], ALU.mult))
                    own.wait()
                    for h in range(GQA):
                        for br, (a, m) in enumerate(((0, n), (512, n), (1024, NC_P))):
                            v = PBUF[u % 2][:, h, a:a + m]
                            dve.tensor_scalar(v, v, FAC[:, u % 2, 3 * h + br:3 * h + br + 1], None, ALU.mult).then_inc(s_pn, 1)

            dve.wait_ge(s_pv, 8)
            own.tick(dve.memset(QP, 0.0))
            own.tick(dve.memset(PEN, 0.0))
            for kv in range(KV):
                for g in range(GQA):
                    own.tick(dve.tensor_copy(QA[:, kv, :].rearrange("p (b g t) -> p b g t", b=NB, g=GQA)[:, :, g, :],
                                             C[:, kv * GQA + g, SEQ:TOK].rearrange("p (b t) -> p b t", b=NB)))
            own.wait()
            diag = bass.AP(RB, 256, [[KT * TOK, P], [NB * P, KV], [P + 16, NB], [1, 16]])
            dve.tensor_copy(diag, QA.rearrange("p k (b r) -> p k b r", b=NB)).then_inc(s_q, 1)
            zeros = cst("mask")[:, 4:4 + NC_S]
            for kv in range(KV):
                dve.wait_ge(s_s1, kv + 1)
                own.tick(dve.tensor_tensor_reduce(PSC[:, kv, 0, :], PS[:, kv, 0:NC_S], zeros, 1.0, NEG, ALU.add, ALU.max, SMC[:, kv:kv + 1]))
                own.tick(dve.tensor_tensor_reduce(PSS[:, kv, PAST:PAST + SAMP], PS[:, kv, 64:96], cst("nmask"), 1.0, NEG, ALU.add, ALU.max,
                                                  SMS[:, kv, 2:3]))
                own.tick(dve.tensor_tensor_reduce(PSW[:, kv, WIN:WIN + SAMP], PS[:, kv, 96:128], cst("nmask"), 1.0, NEG, ALU.add, ALU.max,
                                                  SMW[:, kv, 1:2]))
            own.wait()
            dve.tensor_scalar(SNM[:, 0:2], SMC, -SCALE, None, ALU.mult).then_inc(s_smx, 1)
            dve.wait_ge(s_se, 2)
            own.step(dve.tensor_scalar(SFC[:, 0:2], SSM[:, 0:2], 1e-30, None, ALU.max))
            own.step(dve.reciprocal(SFC[:, 0:2], SFC[:, 0:2]))
            for kv in range(KV):
                own.step(dve.tensor_scalar(PSC[:, kv, 0, :], PSC[:, kv, 0, :], SFC[:, kv:kv + 1], None, ALU.mult))
                dve.wait_ge(s_gs, 2)
                ins = dve.tensor_scalar(PSC[:, kv, 1, :], PSC[:, kv, 0, :], GSMP[:, kv, 0:1], None, ALU.mult)
                if kv == 0:
                    own.step(ins)
            ins.then_inc(s_ss_, 1)
            turned_tiles("s_cmp", s_job)
            dve.wait_ge(s_im, 2)
            dve.tensor_copy(IMP, PS[:, 2, 0:64].rearrange("p (k j) -> p k j", k=KV)[:, :, 0:N_SEL]).then_inc(s_imr, 1)
            dve.wait_ge(s_im, 4)
            imp = PS[:, 3, 0:64].rearrange("p (k j) -> p k j", k=KV)[:, :, 1:N_SEL - 2]
            own.step(dve.tensor_reduce(SMN, imp, AX_X, ALU.min))
            for kv in range(KV):
                own.tick(dve.scalar_tensor_tensor(out=SEQL[:, kv, 0, :], in0=imp[:, kv, :], scalar=SMN[:, kv:kv + 1], in1=cst("jidx"),
                                                  op0=ALU.is_equal, op1=ALU.mult))
            own.wait()
            own.step(dve.tensor_reduce(SJM, SEQL[:, :, 0, :], AX_X, ALU.max))
            for kv in range(KV):
                ins = dve.tensor_scalar(PEN[:, kv, 1:N_SEL - 2], cst("jidx"), SJM[:, kv:kv + 1], NEG, ALU.is_equal, ALU.mult)
                if kv == 0:
                    own.tick(ins)
            ins.then_inc(s_imr, 1)
            for b in range(NB):
                if b >= 2:
                    dve.wait_ge(s_kt, b - 1)
                for k in range(jobs["s_win"] + 2 * b, jobs["s_win"] + 2 * b + 2):
                    turned_tile(k, s_job)
            dve.wait_ge(s_kt, NB)
            for kv in range(KV):
                own.tick(dve.tensor_tensor_reduce(PSW[:, kv, 0:WIN], PS[:, 4 + kv, :], cst("mask")[:, 0:WIN], 1.0, NEG, ALU.add, ALU.max,
                                                  SMW[:, kv, 0:1]))
            for b in range(NB):
                dve.wait_ge(s_kt, NB + b)
                for k in range(jobs["s_sel"] + 4 * b, jobs["s_sel"] + 4 * b + 4):
                    turned_tile(k, s_job)
            dve.wait_ge(s_kt, 2 * NB)
            dve.wait_ge(s_imr, 2)
            for kv in range(KV):
                for h in range(2):
                    pen = PEN[:, kv, 8 * h:8 * h + 8].unsqueeze(2).broadcast_to([P, 8, SEL])
                    own.tick(dve.tensor_tensor_reduce(PSS[:, kv, 512 * h:512 * (h + 1)].rearrange("p (s k) -> p s k", s=8),
                                                      PS[:, 2 * kv + h, :].rearrange("p (s k) -> p s k", s=8), pen, 1.0, NEG, ALU.add, ALU.max,
                                                      SMS[:, kv, h:h + 1]))
            own.wait()
            own.tick(dve.tensor_reduce(SNM[:, 2:4], SMS, AX_X, ALU.max))
            own.step(dve.tensor_reduce(SNM[:, 4:6], SMW, AX_X, ALU.max))
            dve.tensor_scalar(SNM[:, 2:6], SNM[:, 2:6], -SCALE, None, ALU.mult).then_inc(s_smx, 1)
            dve.wait_ge(s_se, 6)
            own.step(dve.tensor_scalar(SFC[:, 2:6], SSM[:, 2:6], 1e-30, None, ALU.max))
            own.step(dve.reciprocal(SFC[:, 2:6], SFC[:, 2:6]))
            own.tick(dve.tensor_tensor(SFC[:, 2:4], SFC[:, 2:4], GSMP[:, :, 1], ALU.mult))
            own.step(dve.tensor_tensor(SFC[:, 4:6], SFC[:, 4:6], GSMP[:, :, 2], ALU.mult))
            for kv in range(KV):
                own.tick(dve.tensor_scalar(PSS[:, kv, :], PSS[:, kv, :], SFC[:, 2 + kv:3 + kv], None, ALU.mult))
                ins = dve.tensor_scalar(PSW[:, kv, :], PSW[:, kv, :], SFC[:, 4 + kv:5 + kv], None, ALU.mult)
                if kv == 0:
                    own.step(ins)
            own.wait()
            ins.then_inc(s_ss_, 1)
            turned_tiles("s_p", s_job)
            for b in range(NB):
                dve.wait_ge(s_so, b + 1)
                for kv in range(KV):
                    ins = dve.tensor_copy(C[:, kv * GQA:(kv + 1) * GQA, SEQ + b * NT:SEQ + (b + 1) * NT],
                                          PS[:, 2 * (b % 2) + kv, 16 * b:16 * b + 16].rearrange("p (g t) -> p g t", g=GQA))
                    if kv == 0:
                        own.tick(ins)
                ins.then_inc(s_sor, 1)

            inverse_root()
            normed(ATT // P, lambda kt: MIX[:, kt, :], lambda kt: C[:, kt, :], lambda kt: VEC[:, kt, 5:6])

            def residual(n, pg, used):
                with dve.Fori(0, n) as i:
                    for j in range(4):
                        dve.wait_ge(s_used[j], i + used)
                        x = XT[:, ds(i * 4 + j, 1), :].rearrange("p o (h t) -> p (o h) t", h=2)
                        dve.tensor_tensor(x, PAIR[j], x, ALU.add).then_inc(s_ps[j], 1)

            dve.wait_ge(s_mrt, 1)
            own.step(dve.reciprocal(MRI, MRT))
            for tt in range(2):
                dve.tensor_scalar(MR[tt], MR[tt], MRI[:, tt:tt + 1], None, ALU.mult).then_inc(s_mn, 1)
            residual(4, PGR["out"], SGR["out"] + 1)
            dve.wait_ge(s_h, HBASE["mem"])
            for k in range(jobs["memr"], end_of("memr")):
                if k % 2 == 1:
                    dve.wait_ge(s_tr, k + 1)
                    dst, src = mem_job(k)[0]
                    m = (k - jobs["memr"]) % 4
                    dve.tensor_tensor(dst, src, VEC[:, 4 * m:4 * m + 4, 2:3].broadcast_to([P, 4, P]), ALU.mult).then_inc(s_te[1], 1)
            turned_tiles("memk", mem_job)
            inverse_root()
            turned(dve, end_of("memr"))
            normed(KT, lambda kt: HTL[:, kt, :], lambda kt: XT[:, kt, :], lambda kt: VEC[:, kt, 1:2])
            for u in range(QB + 1):
                if u < QB:
                    dve.wait_ge(s_msc, u + 1)
                    sc = PS[:, 2 * (u % 2):2 * (u % 2) + 2, :].rearrange("p b (a n) -> p b a n", a=2)
                    own.step(dve.tensor_reduce(MMX[:, u % 2, :].rearrange("p (b a) -> p b a", b=2), sc, AX_X, ALU.max))
                    dve.tensor_scalar(MNM[:, u % 2, :], MMX[:, u % 2, :], -SCALE, None, ALU.mult).then_inc(s_mnm, 1)
                if u:
                    if u >= 2:
                        dve.wait_ge(s_mpv, u - 1)
                    for k in range(jobs["mp"] + 2 * (u - 1), jobs["mp"] + 2 * u):
                        turned_tile(k, mem_job)
                if u < QB:
                    dve.wait_ge(s_mex, u + 1)
                    own.step(dve.reciprocal(MFC[:, u % 2, :], MSU[:, u % 2, :]))
                    dve.tensor_tensor(PMB[u % 2], PMB[u % 2], MFC[:, u % 2, :].unsqueeze(2).broadcast_to([P, MH, NMEM]), ALU.mult).then_inc(s_mpn, 1)
            own.step(dve.memset(QMP, 0.0))
            diag = bass.AP(RF, 3072, [[KT * TOK, P], [NB * SAMP, MH], [SAMP + NT, NB], [1, NT]])
            dve.tensor_copy(diag, QM[:, :, SEQ:TOK].rearrange("p h (b t) -> p h b t", b=NB)).then_inc(s_qmp, 1)
            for b in range(NB):
                if b >= 2:
                    dve.wait_ge(s_msc, QB + b - 1)
                for k in (jobs["ms"] + 2 * b, jobs["ms"] + 2 * b + 1):
                    turned_tile(k, mem_job)
            dve.wait_ge(s_msc, QB + NB)
            own.step(dve.tensor_reduce(MMX[:, 0, 0:1], PS[:, 0, 0:NMEM], AX_X, ALU.max))
            dve.tensor_scalar(MNM[:, 0, 0:1], MMX[:, 0, 0:1], -SCALE, None, ALU.mult).then_inc(s_mnm, 1)
            dve.wait_ge(s_mex, QB + 1)
            own.step(dve.reciprocal(MFC[:, 0, 0:1], MSU[:, 0, 0:1]))
            dve.tensor_scalar(PMS, PMS, MFC[:, 0, 0:1], None, ALU.mult).then_inc(s_mpn, 1)
            turned_tiles("msp", mem_job)
            for m in range(4):
                for j in range(4):
                    if j < 3:
                        dve.wait_ge(s_mop, 3 * m + j + 1)
                    else:
                        dve.wait_ge(s_used[m], SGR["mo"] + 1)
                    dve.tensor_tensor(halves(XT[:, 4 * m + j, :]), PAIR[j], halves(XT[:, 4 * m + j, :]), ALU.add).then_inc(s_ps[j], 1)

            for t in range(2):
                own.step(dve.memset(GX[t][:, 0:2], 0.0))
            turned_tiles("ffp", ffp_job)
            inverse_root()
            normed(KT, lambda kt: HTL[:, kt, :], lambda kt: XT[:, kt, :], lambda kt: VEC[:, kt, 3:4])
            turned(dve, end_of("ffp"))
            STEPS = 2 * 7
            dve.wait_ge(s_out, 16 * 5)
            for f0, n, gu, gd in ffn_plan:
                with dve.Fori(0, n // 2) as i:
                    loop = Chain(dve, s_fl, i * STEPS + f0 * 7)
                    for t in range(2):
                        f = i * 2 + (f0 + t)
                        E, S, W = GX[t][:, 0:2 + SEQ], GX[t][:, 2 + SEQ:].rearrange("p (b t) -> p b t", b=NB), FWT[t]
                        Y, YS = FC[t][:, 0:SEQ], FC[t][:, SEQ:TOK].rearrange("p (b t) -> p b t", b=NB)
                        loop.tick(dve.tensor_copy(W, FP[:, ds(f, 1), :].rearrange("p o c -> p (o c)")))
                        loop.step(dve.tensor_copy(S[:, :, 0:2], FP[:, ds(f, 1), 0:16].rearrange("p o (b t) -> p (o b) t", b=NB)))
                        dve.wait_ge(s_gx, f + 1)
                        loop.tick(dve.tensor_scalar(Y, E[:, 0:SEQ], W[:, 16:17], W[:, 19:20], ALU.mult, ALU.add))
                        loop.step(dve.tensor_scalar(YS, S[:, :, 0:NT], W[:, 16:17], W[:, 19:20], ALU.mult, ALU.add))
                        for w in range(1, FW):
                            loop.tick(dve.scalar_tensor_tensor(out=Y, in0=E[:, w:w + SEQ], scalar=W[:, 16 + w:17 + w], in1=Y, op0=ALU.mult, op1=ALU.add))
                            ins = dve.scalar_tensor_tensor(out=YS, in0=S[:, :, w:w + NT], scalar=W[:, 16 + w:17 + w], in1=YS, op0=ALU.mult, op1=ALU.add)
                            if w < FW - 1:
                                loop.step(ins)
                            else:
                                ins.then_inc(s_fc, 1)
                        dve.wait_ge(s_fs, f + 1)
                        dve.wait_ge(s_used[2 * t + 1], i + (SGR["ffn"] + gu + 1))
                        a = AT[:, ds(i * 2 + t, 1), :].rearrange("p o (h t) -> p (o h) t", h=2)
                        dve.tensor_tensor(a, PAIR[2 * t + 1], halves(FC[t]), ALU.mult).then_inc(s_ps[2 * t + 1], 1)
                residual(4, PGR["ffn"] + gd, SGR["ffn"] + gd + 1)
            turned_tiles("ffs", ffs_job)
            inverse_root()
            normed(KT, lambda kt: HTL[:, kt, :], lambda kt: XT[:, kt, :], lambda kt: VEC[:, kt, 4:5])
            turned_tiles("y", y_job)

        @block.gpsimd
        def _(pool):
            pool.memset(ONES[:, :], 1.0).then_inc(s_ones, 1)
            stores = [0]

            def store(dst, src, s=s_out):
                pool.dma_start(dst, src).then_inc(s, 16)
                if s is s_out:
                    stores[0] += 1

            for n, o in (("cache_k_win", 16), ("cache_v_win", 17)):
                store(O[o][0, :, 0:WIN - NT], A[n][0, :, NT:WIN])
            store(O[18][0, :, 0:PREV - NT, :], A["state_conv"][0, :, NT:PREV, :])
            turned(pool, end_of("kvtok"))
            for t in range(6):
                store(O[2 + t][0, 0].rearrange("(a p) k d -> p a k d", p=P), TOKM[:, 0:4, 2 * t:2 * t + 2, :], s_tok)
                rows = TOKM[0:SAMP, 4, 2 * t:2 * t + 2, :]
                if t < 4:
                    store(O[12 + t][0].rearrange("b t k d -> (b t) k d"), rows, s_tok)
                else:
                    for b in range(NB):
                        store(O[12 + t][0, b, WIN - NT:WIN], TOKM[b * NT:(b + 1) * NT, 4, 2 * t:2 * t + 2, :], s_tok)
            turned(pool, end_of("ucap"))
            store(O[8][0, 0], UR[0][0:PREV, :], s_tok)
            for b in range(NB):
                store(O[18][0, b, PREV - NT:PREV, :], UR[1][b * NT:(b + 1) * NT, :], s_tok)
            for k, dst in enumerate((KMT, VMT)):
                pool.wait_ge(s_mke, k + 1)
                store(O[10 + k][0, 0].rearrange("(a p) h d -> p a (h d)", p=P), dst)
            turned(pool, end_of("ffs"))
            store(O[9][0, 0], FSR[0:2, :])
            store(O[19][0].rearrange("b t c -> (b t) c"), FSR[2:18, :])
            for tt in range(5):
                turned(pool, jobs["y"] + 4 * (tt + 1))
                store(O[0][0, tt * P:(tt + 1) * P, :] if tt < 4 else O[1].rearrange("b t d -> (b t) d"), YR[tt][0:P if tt < 4 else SAMP, :])
            pool.wait_ge(s_tok, 16 * N_TOK)
            pool.wait_ge(s_out, 16 * stores[0])


_INS = ['x_prompt', 'x_sample', 'cache_k_cmp', 'cache_v_cmp', 'cache_k_sel', 'cache_v_sel', 'cache_k_win', 'cache_v_win',
        'state_conv', 'state_ffn_conv', 'cache_mem_k', 'cache_mem_v', 'page_table', 'mem_prompt',
        'norm_mix_g', 'w_in', 'b_gate', 'cmp_k_pe', 'cmp_k_w1', 'cmp_k_b1', 'cmp_k_w2', 'cmp_v_pe', 'cmp_v_w1', 'cmp_v_b1',
        'cmp_v_w2', 'conv_w', 'conv_b', 'conv_ln_g', 'conv_ln_b', 'grp_norm_attn_g', 'grp_norm_conv_g', 'w_out',
        'norm_mem_g', 'mem_norm_g', 'w_mq', 'w_mk', 'w_mv', 'w_mo', 'norm_ffn_g', 'w_ffn_gate', 'w_ffn_up', 'ffn_conv_w',
        'ffn_conv_b', 'w_ffn_down', 'norm_final_g']
_OUTS = ([(1, SEQ, D), (NB, NT, D)] + [(1, 1, SEQ, KV, DH)] * 6 + [(1, 1, PREV, CCH), (1, 1, FW - 1, FF)]
         + [(1, 1, NMEM, MH, DH)] * 2 + [(1, NB, NT, KV, DH)] * 4 + [(1, NB, WIN, KV, DH)] * 2
         + [(1, NB, PREV, CCH), (1, NB, FW - 1, FF)])


def kernel(**inputs):
    import concourse.bacc as bacc
    from concourse.bass_utils import run_bass_kernel_spmd

    nc = bacc.Bacc("TRN2", target_bir_lowering=False, num_devices=1)
    consts, _, gate_rows = constants()
    given = {n: np.ascontiguousarray(inputs[n]) for n in _INS}
    given["consts"], given["gate_rows"] = consts, gate_rows
    arrays, A = {}, {}
    for n, a in given.items():
        arrays[f"in_{n}"] = a
        A[n] = nc.dram_tensor(f"in_{n}", a.shape, mybir.dt.from_np(a.dtype), kind="ExternalInput").ap()
    O = [nc.dram_tensor(f"out_{i}", s, F32, kind="ExternalOutput").ap() for i, s in enumerate(_OUTS)]
    hybrid_step(nc, A, O)
    r = run_bass_kernel_spmd(nc, [arrays], core_ids=[0])
    return tuple(r.results[0][f"out_{i}"] for i in range(len(_OUTS)))
```
